# Optimizing a Trainium2 kernel written in Bass

```python
import math
import jax, jax.numpy as jnp
from jax import lax
import numpy as np

D_MODEL = 1024
BATCH = 1
SEQ = 512
DEPTH = 1

HEAD_DIM = 64
MIX_WIDTH = D_MODEL
SG_WIDTH = MIX_WIDTH // 2
FOX_WIDTH = MIX_WIDTH - SG_WIDTH
SG_HEADS = SG_WIDTH // HEAD_DIM
FOX_HEADS = FOX_WIDTH // HEAD_DIM
CHUNK = 128
Q_BLOCK = 128
IN_COLS = 2 * SG_WIDTH + 3 * FOX_WIDTH + FOX_HEADS
PEER_HEADS = 8
N_KEYS = 128
N_EXPERTS = N_KEYS * N_KEYS
PEER_TOPK = 16
D_KEY = 256
D_HALF = D_KEY // 2
TOKEN_BLOCK = 128
EPS = 1e-6

kernel_name = "hybrid_sgu_fox_peer_adaln"

def rms_norm(x, g):
    xf = x.astype(jnp.float32)
    y = xf * lax.rsqrt(jnp.mean(xf * xf, axis=-1, keepdims=True) + EPS)
    return (y * g.astype(jnp.float32)).astype(x.dtype)

def head_rms_norm(x, g, n_heads):
    b, s, w = x.shape
    xf = x.astype(jnp.float32).reshape(b, s, n_heads, w // n_heads)
    y = xf * lax.rsqrt(jnp.mean(xf * xf, axis=-1, keepdims=True) + EPS)
    return (y.reshape(b, s, w) * g.astype(jnp.float32)).astype(x.dtype)

def modulate(h, shift, scale):
    return h * (1.0 + scale[:, None, :]) + shift[:, None, :]

def spatial_gating(z_u, z_v, ln_g, ln_b, w_s, b_s):
    b, s, _ = z_v.shape
    vf = z_v.astype(jnp.float32).reshape(b, s, SG_HEADS, HEAD_DIM)
    mu = jnp.mean(vf, axis=-1, keepdims=True)
    var = jnp.mean(jnp.square(vf - mu), axis=-1, keepdims=True)
    vn = (vf - mu) * lax.rsqrt(var + EPS)
    vn = vn * ln_g.astype(jnp.float32).reshape(SG_HEADS, HEAD_DIM) + ln_b.astype(jnp.float32).reshape(SG_HEADS, HEAD_DIM)
    vn = vn.astype(z_v.dtype).reshape(b, s // CHUNK, CHUNK, SG_HEADS, HEAD_DIM)
    causal = jnp.tril(jnp.ones((CHUNK, CHUNK), dtype=w_s.dtype))
    w = w_s * causal[None]
    mixed = jnp.einsum('hts,bcshd->bcthd', w, vn)
    mixed = mixed + jnp.transpose(b_s)[None, None, :, :, None]
    return z_u * mixed.reshape(b, s, SG_WIDTH)

def forgetting_attention(q, k, v, f_logit):
    b, s, h, dh = q.shape
    nb = s // Q_BLOCK
    cum = jnp.cumsum(jax.nn.log_sigmoid(f_logit.astype(jnp.float32)), axis=1)
    cum_k = jnp.transpose(cum, (0, 2, 1))
    q_blocks = q.reshape(b, nb, Q_BLOCK, h, dh).transpose(1, 0, 2, 3, 4)
    cum_q = cum.reshape(b, nb, Q_BLOCK, h).transpose(1, 0, 3, 2)
    k_pos = jnp.arange(s)
    scale = HEAD_DIM ** -0.5

    def one_block(args):
        qi, cqi, i = args
        logits = jnp.einsum('bqhd,bkhd->bhqk', qi, k).astype(jnp.float32) * scale
        logits = logits + cqi[..., :, None] - cum_k[:, :, None, :]
        q_pos = i * Q_BLOCK + jnp.arange(Q_BLOCK)
        mask = k_pos[None, :] <= q_pos[:, None]
        logits = jnp.where(mask[None, None], logits, -jnp.inf)
        p = jax.nn.softmax(logits, axis=-1).astype(v.dtype)
        return jnp.einsum('bhqk,bkhd->bqhd', p, v)

    out = lax.map(one_block, (q_blocks, cum_q, jnp.arange(nb)))
    return out.transpose(1, 0, 2, 3, 4).reshape(b, s, h * dh)

def token_mixer(h, w_in, b_f, sg_ln_g, sg_ln_b, sg_w, sg_b, out_g_sg, out_g_fox, w_out):
    b, s, _ = h.shape
    proj = h @ w_in
    c0 = SG_WIDTH
    c1 = 2 * SG_WIDTH
    c2 = c1 + FOX_WIDTH
    c3 = c2 + FOX_WIDTH
    c4 = c3 + FOX_WIDTH
    z_u = jax.nn.gelu(proj[..., :c0], approximate=False)
    z_v = jax.nn.gelu(proj[..., c0:c1], approximate=False)
    q = proj[..., c1:c2].reshape(b, s, FOX_HEADS, HEAD_DIM)
    k = proj[..., c2:c3].reshape(b, s, FOX_HEADS, HEAD_DIM)
    v = proj[..., c3:c4].reshape(b, s, FOX_HEADS, HEAD_DIM)
    f_logit = proj[..., c4:] + b_f
    y_sg = spatial_gating(z_u, z_v, sg_ln_g, sg_ln_b, sg_w, sg_b)
    y_fox = forgetting_attention(q, k, v, f_logit)
    y = jnp.concatenate([head_rms_norm(y_sg, out_g_sg, SG_HEADS),
                         head_rms_norm(y_fox, out_g_fox, FOX_HEADS)], axis=-1)
    return y @ w_out

def peer_ffn(h, w_query, sub_keys, expert_u, expert_v):
    b, s, d = h.shape
    t = b * s
    xt = h.reshape(t, d)
    q = (xt @ w_query).reshape(t, PEER_HEADS, 2, D_HALF)
    scores = jnp.einsum('thpd,hpnd->thpn', q, sub_keys).astype(jnp.float32)
    sv, si = lax.top_k(scores, PEER_TOPK)
    cand_s = (sv[:, :, 0, :, None] + sv[:, :, 1, None, :]).reshape(t, PEER_HEADS, PEER_TOPK * PEER_TOPK)
    cand_i = (si[:, :, 0, :, None] * N_KEYS + si[:, :, 1, None, :]).reshape(t, PEER_HEADS, PEER_TOPK * PEER_TOPK)
    top_s, pos = lax.top_k(cand_s, PEER_TOPK)
    idx = jnp.take_along_axis(cand_i, pos, axis=-1)
    gate = jax.nn.softmax(top_s, axis=-1).astype(h.dtype)
    nblk = t // TOKEN_BLOCK
    n_sel = PEER_HEADS * PEER_TOPK
    x_blocks = xt.reshape(nblk, TOKEN_BLOCK, d)
    idx_blocks = idx.reshape(nblk, TOKEN_BLOCK, n_sel)
    gate_blocks = gate.reshape(nblk, TOKEN_BLOCK, n_sel)

    def one_block(args):
        xi, ii, gi = args
        u = jnp.take(expert_u, ii, axis=0)
        a = jnp.einsum('ted,td->te', u, xi)
        w = gi * jax.nn.gelu(a, approximate=False)
        vv = jnp.take(expert_v, ii, axis=0)
        return jnp.einsum('te,ted->td', w, vv)

    out = lax.map(one_block, (x_blocks, idx_blocks, gate_blocks))
    return out.reshape(b, s, d)

def setup_inputs(seed: int = 0) -> dict:
    key = jax.random.key(seed)
    ks = jax.random.split(key, 24)
    f32 = jnp.float32
    D = D_MODEL

    def nrm(k, shape, scale):
        return jax.random.normal(k, shape, f32) * scale

    x = jax.random.normal(ks[0], (BATCH, SEQ, D), f32)
    c = jax.random.normal(ks[1], (BATCH, D), f32)
    w_ada = nrm(ks[2], (DEPTH, D, 6 * D), 0.5 * D ** -0.5)
    b_ada = nrm(ks[3], (DEPTH, 6 * D), 0.02)
    norm1_g = 1.0 + nrm(ks[4], (DEPTH, D), 0.02)
    w_in = nrm(ks[5], (DEPTH, D, IN_COLS), D ** -0.5)
    b_f = jax.random.uniform(ks[6], (DEPTH, FOX_HEADS), f32, minval=1.0, maxval=5.0)
    sg_ln_g = 1.0 + nrm(ks[7], (DEPTH, SG_WIDTH), 0.02)
    sg_ln_b = nrm(ks[8], (DEPTH, SG_WIDTH), 0.02)
    sg_w = nrm(ks[9], (DEPTH, SG_HEADS, CHUNK, CHUNK), CHUNK ** -0.5)
    sg_b = 1.0 + nrm(ks[10], (DEPTH, SG_HEADS, CHUNK), 0.1)
    out_g_sg = 1.0 + nrm(ks[11], (DEPTH, SG_WIDTH), 0.02)
    out_g_fox = 1.0 + nrm(ks[12], (DEPTH, FOX_WIDTH), 0.02)
    w_out = nrm(ks[13], (DEPTH, MIX_WIDTH, D), MIX_WIDTH ** -0.5)
    norm2_g = 1.0 + nrm(ks[14], (DEPTH, D), 0.02)
    w_query = nrm(ks[15], (DEPTH, D, PEER_HEADS * D_KEY), D ** -0.5)
    sub_keys = nrm(ks[16], (DEPTH, PEER_HEADS, 2, N_KEYS, D_HALF), D_HALF ** -0.5)
    expert_u = nrm(ks[17], (DEPTH, N_EXPERTS, D), D ** -0.5)
    expert_v = nrm(ks[18], (DEPTH, N_EXPERTS, D), PEER_HEADS ** -0.5)
    final_g = 1.0 + nrm(ks[19], (D,), 0.02)
    return {"x": x, "c": c, "w_ada": w_ada, "b_ada": b_ada, "norm1_g": norm1_g,
            "w_in": w_in, "b_f": b_f, "sg_ln_g": sg_ln_g, "sg_ln_b": sg_ln_b,
            "sg_w": sg_w, "sg_b": sg_b, "out_g_sg": out_g_sg, "out_g_fox": out_g_fox,
            "w_out": w_out, "norm2_g": norm2_g, "w_query": w_query, "sub_keys": sub_keys,
            "expert_u": expert_u, "expert_v": expert_v, "final_g": final_g}

def reference(x, c, w_ada, b_ada, norm1_g, w_in, b_f, sg_ln_g, sg_ln_b, sg_w, sg_b,
              out_g_sg, out_g_fox, w_out, norm2_g, w_query, sub_keys, expert_u, expert_v,
              final_g):
    c_act = jax.nn.silu(c)
    for l in range(DEPTH):
        ada = c_act @ w_ada[l] + b_ada[l]
        shift1, scale1, gate1, shift2, scale2, gate2 = jnp.split(ada, 6, axis=-1)
        h = modulate(rms_norm(x, norm1_g[l]), shift1, scale1)
        mix = token_mixer(h, w_in[l], b_f[l], sg_ln_g[l], sg_ln_b[l], sg_w[l], sg_b[l],
                          out_g_sg[l], out_g_fox[l], w_out[l])
        x = x + gate1[:, None, :] * mix
        h = modulate(rms_norm(x, norm2_g[l]), shift2, scale2)
        ffn = peer_ffn(h, w_query[l], sub_keys[l], expert_u[l], expert_v[l])
        x = x + gate2[:, None, :] * ffn
    return rms_norm(x, final_g)


_drawn_inputs = setup_inputs


def setup_inputs(seed=0):
    import zlib

    import numpy as np

    out = dict(_drawn_inputs(seed))
    spreads = {}
    factors = {'norm1_g': 6.888,
     'sg_ln_g': 8.0,
     'sg_ln_b': 8.0,
     'sg_b': 5.415,
     'out_g_sg': 8.0,
     'out_g_fox': 8.0,
     'norm2_g': 7.22,
     'final_g': 2.829}
    for name, (base, spread) in spreads.items():
        noise = np.random.default_rng([zlib.crc32(name.encode()), seed]).standard_normal(out[name].shape)
        drawn = base * np.exp(spread * noise) if base else spread * noise
        out[name] = __import__('jax').numpy.asarray(drawn.astype(out[name].dtype))
    for name, factor in factors.items():
        out[name] = (out[name] * factor).astype(out[name].dtype)
    return out
```

```python
from contextlib import ExitStack

import concourse.bass as bass
from concourse import mybir

F32 = mybir.dt.float32
U32 = mybir.dt.uint32
ALU = mybir.AluOpType
ACT = mybir.ActivationFunctionType
AX_X = mybir.AxisListType.X

P = 128
SEQ = 512
D = 1024
NT = SEQ // P
KC = D // P
HALF = 512
HEADS = 8
DH = 64
PH = 8
HP = 2 * PH
NKEYS = 128
TOPK = 16
NSEL = PH * TOPK
N_EXPERTS = NKEYS * NKEYS
EPS = 1e-6
MASKED = -1e30
TAKEN = -3e38

RING = 8
ROUNDS = NSEL // RING
SLOTS = 6
DIAGS = RING // 2
V_PE = NSEL // 2

ADA_EARLY = [("ada", g) for g in range(4)]
W_IN = [("w_in", c) for c in ("zv", "v", "zu", "q", "k")]
ADA_LATE = [("ada", g) for g in range(4, 12)]
RESIDENT = [("w_out", 0), ("w_out", 1)] + [("w_query", g) for g in range(4)]
STREAM = ADA_EARLY + W_IN + ADA_LATE + RESIDENT
W_IN_COL = {"zu": 0, "zv": 512, "q": 1024, "k": 1536, "v": 2048}
F_COL = 2560

ATTN = [(qt, h) for qt in range(NT) for h in range(HEADS)]


def plan_banks():
    jobs = [(("ada", g), 4 + g % 2) for g in range(4)]
    jobs += [(("h1T", t, s), 6 + s) for t in range(NT) for s in range(2)]
    proj = [("zv", t) for t in range(NT)] + [("v", t) for t in range(NT)] + [("f",)]
    proj += [("zu", t) for t in range(NT)] + [("q", c) for c in range(4)] + [("k", c) for c in range(4)]
    jobs += [(j, n % 4) for n, j in enumerate(proj)]
    jobs += [(("ada", g), 4 + g % 2) for g in range(4, 12)]
    jobs += [(("cum",), 6)]
    jobs += [(("sgu", b), b) for b in range(4)]
    jobs += [(("S", n), 4 + n % 2) for n in range(len(ATTN))]
    jobs += [(("PT", n), 6 + n % 2) for n in range(len(ATTN))]
    jobs += [(("O", t), t % 2) for t in range(NT)]
    for t in range(NT):
        jobs += [(("yT", t, s), 2 + s) for s in range(2)]
        jobs += [(("mix", t, s), s) for s in range(2)]
        jobs += [(("h2T", t, s), 2 + s) for s in range(2)]
        jobs += [(("qrow", t, g), (4, 5, 0, 1)[g]) for g in range(4)]
        jobs += [(("qT", t, g), (2, 3, 4, 5)[g]) for g in range(4)]
        jobs += [(("score", t, g), g) for g in range(4)]
    place, count = {}, [0] * 8
    for name, b in jobs:
        count[b] += 1
        place[name] = (b, count[b])
    return place


def program(nc, x, cT, w_ada, b_ada, norm1_g, w_in, b_f, sg_ln_g, sg_ln_b, sg_wT, sg_bT,
            out_gT, w_out, norm2_g, w_query, sub_keysT, expert_u, expert_v, final_g, out):
    place = plan_banks()
    slot_of = {name: n % SLOTS for n, name in enumerate(STREAM)}
    load_of = {name: 16 * (n // SLOTS + 1) for n, name in enumerate(STREAM)}

    with ExitStack() as ctx:
        def sb(name, shape, dt=F32):
            return ctx.enter_context(nc.sbuf_tensor(name, shape, dt))

        def sem(name):
            return ctx.enter_context(nc.semaphore(name))

        weights = sb("weights", [P, SLOTS, KC, HALF])
        shared = sb("shared", [P, 8 * D])
        xs = sb("xs", [P, NT, D])
        ada = sb("ada", [P, 6 * D])
        hT = sb("hT", [P, KC, SEQ])
        y = sb("y", [P, NT, D])
        ident = sb("ident", [P, P])
        final_row = sb("final_row", [P, D])
        idx = sb("idx", [P, 2, NSEL], U32)
        gate = sb("gate", [P, NSEL])
        act_w = sb("act_w", [P, NSEL])
        misc = sb("misc", [P, 160])
        idx_slot = sb("idx_slot", [P, 2, RING], U32)

        h1 = shared[:, 0:4 * D].rearrange("p (t d) -> p t d", t=NT)
        q_z = shared[:, 0:4 * D].rearrange("p (h s) -> p h s", h=HEADS)
        kT = shared[:, 4 * D:6 * D].rearrange("p (c s) -> p c s", c=4)
        v_tok = shared[:, 6 * D:8 * D].rearrange("p (t d) -> p t d", t=NT)
        ring = shared[:, :].rearrange("p (r d) -> p r d", r=RING)

        hTf = hT[:, :, :].rearrange("p k s -> p (k s)")
        norm1_row = hTf[:, 0:D]
        sgw = hTf[:, 0:D].rearrange("p (h t) -> p h t", h=HEADS)
        p_exp = hTf[:, D:2 * D].rearrange("p (b s) -> p b s", b=2)
        p_T = hTf[:, 2 * D:3 * D].rearrange("p (b s) -> p b s", b=2)
        ncum = hTf[0:HEADS, 3 * D:3 * D + SEQ]
        causal = hTf[:, 3 * D + SEQ:3 * D + SEQ + P]
        yT = hTf[:, 0:D].rearrange("p (k t) -> p k t", k=KC)
        h2T = hTf[:, D:2 * D].rearrange("p (k t) -> p k t", k=KC)
        qT = hTf[:, 0:2 * D].rearrange("p (g t) -> p g t", g=HP)
        cand = hTf[:, 0:2 * D].rearrange("p (h e) -> p h e", h=PH)
        squares = hTf[:, 2 * D:3 * D]
        qrow = hTf[:, 2 * D:4 * D]
        scores = hTf[:, 2 * D:4 * D].rearrange("p (g n) -> p g n", g=HP)
        pos_a = hTf[:, 2 * D:2 * D + NSEL]
        pos_b = hTf[:, 2 * D + NSEL:2 * D + 2 * NSEL]
        sel_i = hTf[:, 2 * D + 2 * NSEL:2 * D + 3 * NSEL]
        sel_j = hTf[:, 2 * D + 3 * NSEL:2 * D + 4 * NSEL]
        pos_u = hTf[:, 2 * D + 4 * NSEL:2 * D + 5 * NSEL].bitcast(U32)

        def row(n):
            return ada[:, n * D:(n + 1) * D]
        shift1, scale1, gate1, shift2, scale2, gate2 = (row(n) for n in range(6))
        ln_g, ln_b = ada[:, 0:HALF], ada[:, HALF:D]
        v_sq = ada[:, D:2 * D]
        norm2_row = ada[:, D:2 * D]
        keysT = ada[:, 0:2 * D].rearrange("p (g n) -> p g n", g=HP)
        onehot = ada[:, 0:D].rearrange("p (s a) -> p s a", a=TOPK)
        top_v = ada[:, D:D + 256].rearrange("p (g k) -> p g k", g=HP)
        top_i = ada[:, D + 256:D + 512].bitcast(U32).rearrange("p (g k) -> p g k", g=HP)
        top_f = ada[:, D + 512:D + 768].rearrange("p (g k) -> p g k", g=HP)
        best_v = ada[:, D + 768:D + 896].rearrange("p (h k) -> p h k", h=PH)
        best_p = ada[:, D + 896:D + 1024].bitcast(U32).rearrange("p (h k) -> p h k", h=PH)
        diag = ada[:, 2 * D:2 * D + DIAGS * P].rearrange("p (b t) -> p b t", b=DIAGS)

        tri = act_w[:, :]
        c_col, c_act, c_exp = misc[:, 0:8], misc[:, 8:16], misc[:, 16:24]
        out_g = misc[:, 24:32]
        sgb = misc[:, 32:40]
        bf_row = misc[:, 40:48]
        iota16 = misc[:, 48:64]
        x_ss, x_rms = misc[:, 64:68], misc[:, 68:72]
        y_var, y_rms = misc[:, 72:88], misc[:, 88:104]
        x1_ss, x1_rms = misc[:, 104:105], misc[:, 105:106]
        x2_ss, x2_rms = misc[:, 106:107], misc[:, 107:108]
        gate_sum = misc[:, 108:116]
        logit = idx[:, 0, 0:32].bitcast(F32)
        lsg_e = idx[:, 0, 32:64].bitcast(F32)
        lsg = idx[:, 0, 64:96].bitcast(F32)
        nmax = idx[:, 0, 96:128].bitcast(F32)
        rsum = idx[:, 1, 0:32].bitcast(F32)
        v_mean = idx[:, 1, 32:64].bitcast(F32)
        v_var = idx[:, 1, 64:96].bitcast(F32)
        o_scale = idx[:, 1, 96:128].bitcast(F32)
        f_w = gate[:, 0:64].rearrange("p (k f) -> p k f", k=KC)
        iota_u = gate[:, 64:80].bitcast(U32)
        ones = gate[:, 80:81].broadcast_to([P, P])

        bank = [ctx.enter_context(nc.psum_tensor(f"bank{b}", [P, HALF], F32)) for b in range(8)]

        weight_in = [sem(f"weight_in{s}") for s in range(SLOTS)]
        full = [sem(f"bank{b}_full") for b in range(8)]
        read = [sem(f"bank{b}_read") for b in range(8)]
        gathered = [sem(f"gathered{r}") for r in range(RING)]
        x_in, c_in, small_in, norm1_in = sem("x_in"), sem("c_in"), sem("small_in"), sem("norm1_in")
        b_ada_in, norm2_in, ln_in, sgw_in = sem("b_ada_in"), sem("norm2_in"), sem("ln_in"), sem("sgw_in")
        final_in, fw_in, keys_in, stored = sem("final_in"), sem("fw_in"), sem("keys_in"), sem("stored")
        made, causal_made, sgw_masked, qz_zero = sem("made"), sem("causal_made"), sem("sgw_masked"), sem("qz_zero")
        c_exped = sem("c_exped")
        ada_summed = sem("ada_summed")
        a1_done, a2_done, h1_ready = sem("a1_done"), sem("a2_done"), sem("h1_ready")
        x_squared, x_mean, x_root = sem("x_squared"), sem("x_mean"), sem("x_root")
        f_abs, f_exp, f_plus, f_log, f_done = sem("f_abs"), sem("f_exp"), sem("f_plus"), sem("f_log"), sem("f_done")
        v_var_ready, v_root, v_norm = sem("v_var_ready"), sem("v_root"), sem("v_norm")
        neg_max, pT_used = sem("neg_max"), sem("pT_used")
        w_out_gated = sem("w_out_gated")
        y_squared, y_mean, y_root, y_ready = sem("y_squared"), sem("y_mean"), sem("y_root"), sem("y_ready")
        x1_squared, x1_mean, x1_root, h2_ready = sem("x1_squared"), sem("x1_mean"), sem("x1_root"), sem("h2_ready")
        best_ready, gate_exp, topk_done = sem("best_ready"), sem("gate_exp"), sem("topk_done")
        granted, idx_staged = sem("slot_granted"), sem("idx_staged")
        dot_done, gelu_done, w_ready = sem("dot_done"), sem("gelu_done"), sem("w_ready")
        diag_granted, diag_ready, v_used, acc_read = sem("diag_granted"), sem("diag_ready"), sem("v_used"), sem("acc_read")
        v_added = sem("v_added")
        x2_ready, x2_squared, x2_mean, x2_root = sem("x2_ready"), sem("x2_squared"), sem("x2_mean"), sem("x2_root")
        out_ready = sem("out_ready")
        v_chain, g_chain = sem("vector_chain"), sem("gpsimd_chain")

        block = ctx.enter_context(nc.Block())

        def wait_full(eng, *name):
            b, n = place[name]
            eng.wait_ge(full[b], n)
            return bank[b]

        def wait_read(eng, *name):
            b, n = place[name]
            eng.wait_ge(read[b], n)

        def release(ins, *name):
            ins.then_inc(read[place[name][0]], 1)

        def group_source(kind, g):
            if kind == "ada":
                src = w_ada[:, g * HALF:(g + 1) * HALF]
            elif kind == "w_in":
                src = w_in[:, W_IN_COL[g]:W_IN_COL[g] + HALF]
            elif kind == "w_out":
                src = w_out[:, g * HALF:(g + 1) * HALF]
            else:
                src = w_query[:, g * HALF:(g + 1) * HALF]
            return src.rearrange("(k p) n -> p k n", p=P)

        def one_row(v):
            return v.rearrange("(a n) -> a n", a=1)

        def on_all(v):
            return one_row(v).broadcast_to([P, v.shape[0]])

        def wait_weights(eng, *name):
            eng.wait_ge(weight_in[slot_of[name]], load_of[name])
            return weights[:, slot_of[name], :, :]

        @block.sync
        def _(sp):
            def load_group(n):
                name = STREAM[n]
                if n >= SLOTS:
                    kind, g = STREAM[n - SLOTS]
                    if kind == "ada":
                        sp.wait_ge(ada_summed, g + 1)
                    else:
                        wait_full(sp, g, 3)
                sp.dma_start(weights[:, slot_of[name], :, :], group_source(*name)).then_inc(weight_in[slot_of[name]], 16)

            sp.dma_start(c_col, cT).then_inc(c_in, 16)
            load_group(0)
            sp.dma_start(xs[:, :, :], x.rearrange("(t p) d -> p t d", p=P)).then_inc(x_in, 16)
            for n in range(1, 4):
                load_group(n)
            sp.dma_start(norm1_row, on_all(norm1_g)).then_inc(norm1_in, 16)
            for n in range(4, SLOTS):
                load_group(n)
            sp.wait_ge(made, 3)
            sp.dma_start(f_w, w_in[:, F_COL:F_COL + HEADS].rearrange("(k p) n -> p k n", p=P)).then_inc(fw_in, 16)
            sp.dma_start(bf_row, on_all(b_f)).then_inc(small_in, 16)
            sp.dma_start(sgb, sg_bT).then_inc(small_in, 16)
            sp.dma_start(out_g, out_gT).then_inc(small_in, 16)
            sp.dma_start(final_row[:, :], on_all(final_g)).then_inc(final_in, 16)
            for n in range(SLOTS, SLOTS + 3):
                load_group(n)
            sp.wait_ge(h1_ready, NT)
            sp.dma_start(ln_g, on_all(sg_ln_g)).then_inc(ln_in, 16)
            sp.dma_start(ln_b, on_all(sg_ln_b)).then_inc(ln_in, 16)
            for n in range(SLOTS + 3, len(STREAM)):
                load_group(n)
                if STREAM[n] == ("ada", 9):
                    sp.wait_ge(v_var_ready, 1)
                    sp.dma_start(norm2_row, on_all(norm2_g)).then_inc(norm2_in, 16)
                    wait_full(sp, "k", 3)
                    sp.dma_start(sgw, sg_wT).then_inc(sgw_in, 16)
            for t in range(NT):
                if t == 0:
                    sp.wait_ge(a2_done, 1)
                else:
                    sp.wait_ge(topk_done, t)
                sp.dma_start(keysT, sub_keysT).then_inc(keys_in, 16)
            for t in range(NT):
                sp.wait_ge(out_ready, t + 1)
                sp.dma_start(out[t * P:(t + 1) * P, :], xs[:, t, :]).then_inc(stored, 16)
            sp.wait_ge(stored, 16 * NT)

        @block.gpsimd
        def _(pool):
            links = [0]

            def link(ins):
                links[0] += 1
                ins.then_inc(g_chain, 1)
                pool.wait_ge(g_chain, links[0])

            link(nc.gpsimd.memset(ada[:, :], 0.0))
            pool.dma_start(ada[0:1, :], one_row(b_ada)).then_inc(b_ada_in, 16)
            link(nc.gpsimd.memset(ident[:, :], 0.0))
            link(nc.gpsimd.memset(gate[:, :], 1.0))
            link(nc.gpsimd.memset(tri, 1.0))
            nc.gpsimd.iota(iota_u, [[1, TOPK]], base=0, channel_multiplier=0).then_inc(made, 1)
            nc.gpsimd.affine_select(out=ident[:, :], in_=ident[:, :], compare_op=ALU.not_equal, fill=1.0,
                                    base=0, pattern=[[-1, P]], channel_multiplier=1).then_inc(made, 1)
            nc.gpsimd.affine_select(out=tri, in_=tri, compare_op=ALU.is_ge, fill=0.0,
                                    base=0, pattern=[[1, P]], channel_multiplier=-1).then_inc(made, 1)
            wait_full(pool, "h1T", 3, 1)
            nc.gpsimd.memset(q_z, 0.0).then_inc(qz_zero, 1)
            wait_full(pool, "k", 3)
            link(nc.gpsimd.memset(causal, 0.0))
            nc.gpsimd.affine_select(out=causal, in_=causal, compare_op=ALU.is_ge, fill=MASKED,
                                    base=0, pattern=[[-1, P]], channel_multiplier=1).then_inc(causal_made, 1)
            pool.wait_ge(sgw_in, 16)
            nc.gpsimd.affine_select(out=sgw, in_=sgw, compare_op=ALU.is_ge, fill=0.0,
                                    base=0, pattern=[[0, HEADS], [1, P]], channel_multiplier=-1).then_inc(sgw_masked, 1)
            wait_read(pool, "ada", 4)
            wait_read(pool, "ada", 5)
            for g in range(2):
                w = wait_weights(pool, "w_out", g)
                for k in range(KC):
                    nc.gpsimd.tensor_tensor(w[:, k, :], w[:, k, :], gate1[:, g * HALF:(g + 1) * HALF],
                                            ALU.mult).then_inc(w_out_gated, 1)

            def dots_used(t, last, r):
                pool.wait_ge(dot_done, t * NSEL + last * RING + r + 1)

            def v_rows_used(t, last, r):
                pool.wait_ge(v_added if r % 2 else v_used, t * V_PE + last * DIAGS + r // 2 + 1)

            def gather_rows(table, t, which, wait_first, wait_used):
                rounds = 2 * ROUNDS * t + which * ROUNDS

                def one_round(i, half, first):
                    nc.gpsimd.tensor_copy(idx_slot[:, half, :], idx[:, t % 2, bass.ds((2 * i + half) * RING, RING)])\
                        .then_inc(idx_staged, 1)
                    pool.wait_ge(idx_staged, rounds + 2 * i + half + 1)
                    for r in range(RING):
                        if first:
                            wait_first(r)
                        else:
                            wait_used(t, 2 * i + half - 1, r)
                        pool.sem_inc(granted, 1)
                        nc.gpsimd.indirect_dma_start(ring[:, r, :], None, table,
                                                     bass.IndirectOffsetOnAxis(idx_slot[:, half, r:r + 1], 0))\
                            .then_inc(gathered[r], 16)

                one_round(0, 0, True)
                one_round(0, 1, False)
                with pool.Fori(1, ROUNDS // 2) as i:
                    one_round(i, 0, False)
                    one_round(i, 1, False)

            for t in range(NT):
                def first_of_u(r):
                    if t == 0:
                        wait_full(pool, "O", NT - 1)
                    else:
                        v_rows_used(t - 1, ROUNDS - 1, r)

                def first_of_v(r):
                    dots_used(t, ROUNDS - 1, r)

                pool.wait_ge(topk_done, t + 1)
                gather_rows(expert_u, t, 0, first_of_u, dots_used)
                gather_rows(expert_v, t, 1, first_of_v, v_rows_used)

        @block.scalar
        def _(act):
            act.wait_ge(c_in, 16)
            nc.scalar.activation(c_exp, c_col, ACT.Exp, scale=-1.0).then_inc(c_exped, 1)
            act.wait_ge(x_in, 16)
            for t in range(NT):
                nc.scalar.activation(y[:, t, :], xs[:, t, :], ACT.Square, accum_out=x_ss[:, t:t + 1]).then_inc(x_squared, 1)
            act.wait_ge(x_mean, 1)
            nc.scalar.activation(x_rms, x_ss, ACT.Sqrt).then_inc(x_root, 1)

            def ada_row(g):
                b = wait_full(act, "ada", g)
                release(nc.scalar.activation(ada[:, g * HALF:(g + 1) * HALF], b[:, :], ACT.Copy), "ada", g)

            def copy_chunks(dst, name, func=ACT.Copy):
                b = wait_full(act, *name)
                release(nc.scalar.activation(dst, b[:, :].rearrange("p (k t) -> p k t", k=4), func), *name)

            for g in range(4):
                ada_row(g)
            act.wait_ge(a1_done, 1)
            for t in range(NT):
                for s in range(2):
                    copy_chunks(hT[:, 4 * s:4 * s + 4, t * P:(t + 1) * P], ("h1T", t, s))
            for t in range(NT):
                b = wait_full(act, "zv", t)
                release(nc.scalar.activation(y[:, t, HALF:D], b[:, :], ACT.Gelu), "zv", t)
            act.wait_ge(f_abs, 1)
            nc.scalar.activation(lsg_e, lsg_e, ACT.Exp, scale=-1.0).then_inc(f_exp, 1)
            act.wait_ge(f_plus, 1)
            nc.scalar.activation(lsg_e, lsg_e, ACT.Ln).then_inc(f_log, 1)
            for t in range(NT):
                b = wait_full(act, "zu", t)
                release(nc.scalar.activation(y[:, t, 0:HALF], b[:, :], ACT.Gelu), "zu", t)
            act.wait_ge(qz_zero, 1)
            for n in range(4):
                b = wait_full(act, "q", n)
                nc.scalar.activation(q_z[0:DH, 2 * n, :], b[0:DH, :], ACT.Copy, scale=DH ** -0.5)
                release(nc.scalar.activation(q_z[DH:P, 2 * n + 1, :], b[DH:P, :], ACT.Copy, scale=DH ** -0.5), "q", n)
            act.wait_ge(v_var_ready, 1)
            nc.scalar.activation(v_var, v_var, ACT.Sqrt).then_inc(v_root, 1)
            for g in range(4, 12):
                ada_row(g)
            b = wait_full(act, "cum")
            release(nc.scalar.activation(ncum, b[0:HEADS, :], ACT.Copy, scale=-1.0), "cum")

            for n, (qt, h) in enumerate(ATTN):
                keys = (qt + 1) * P
                act.wait_ge(neg_max, n + 1)
                if n >= 2:
                    wait_full(act, "PT", n - 2)
                release(nc.scalar.activation(p_exp[:, n % 2, 0:keys], bank[place["S", n][0]][:, 0:keys], ACT.Exp,
                                             bias=nmax[:, n:n + 1], accum_out=rsum[:, n:n + 1]),
                        "S", n)

            def front(t):
                wait_read(act, "O", NT - 1)
                if t:
                    act.wait_ge(topk_done, t)
                nc.scalar.activation(squares, y[:, t, :], ACT.Square).then_inc(y_squared, 1)
                act.wait_ge(y_mean, t + 1)
                nc.scalar.activation(y_rms, y_var, ACT.Sqrt).then_inc(y_root, 1)
                wait_read(act, "mix", t, 1)
                nc.scalar.activation(squares, xs[:, t, :], ACT.Square, accum_out=x1_ss).then_inc(x1_squared, 1)
                act.wait_ge(x1_mean, t + 1)
                nc.scalar.activation(x1_rms, x1_ss, ACT.Sqrt).then_inc(x1_root, 1)
                for s in range(2):
                    copy_chunks(h2T[:, 4 * s:4 * s + 4, :], ("h2T", t, s))
                for g in range(4):
                    b = wait_full(act, "qrow", t, g)
                    release(nc.scalar.activation(qrow[:, g * HALF:(g + 1) * HALF], b[:, :], ACT.Copy), "qrow", t, g)
                for g in range(4):
                    copy_chunks(qT[:, 4 * g:4 * g + 4, :], ("qT", t, g))
                for g in range(4):
                    copy_chunks(scores[:, 4 * g:4 * g + 4, :], ("score", t, g))

            def gate_exps(t):
                act.wait_ge(best_ready, t + 1)
                nc.scalar.activation(gate[:, :], gate[:, :], ACT.Exp).then_inc(gate_exp, 1)

            front(0)
            gate_exps(0)
            for t in range(NT):
                if t + 1 < NT:
                    front(t + 1)
                act.wait_ge(dot_done, (t + 1) * NSEL)
                nc.scalar.activation(act_w[:, :], act_w[:, :], ACT.Gelu).then_inc(gelu_done, 1)
                if t == 0:
                    act.wait_ge(w_out_gated, 2 * KC)
                act.wait_ge(w_ready, t + 1)

                def diagonals(i, first):
                    for n in range(DIAGS):
                        if not first:
                            act.wait_ge(v_used, t * V_PE + DIAGS * (i - 1) + n + 1)
                        act.sem_inc(diag_granted, 1)
                        nc.scalar.activation(diag[:, n, :], ident[:, :], ACT.Copy,
                                             scale=act_w[:, bass.ds(RING * i + 2 * n, 1)]).then_inc(diag_ready, 1)

                if t:
                    act.wait_ge(v_used, t * V_PE)
                diagonals(0, True)
                with act.Fori(1, ROUNDS) as i:
                    diagonals(i, False)
                if t + 1 < NT:
                    gate_exps(t + 1)
                act.wait_ge(x2_ready, t + 1)
                nc.scalar.activation(y[:, t, :], xs[:, t, :], ACT.Square, accum_out=x2_ss).then_inc(x2_squared, 1)
                act.wait_ge(x2_mean, t + 1)
                nc.scalar.activation(x2_rms, x2_ss, ACT.Sqrt).then_inc(x2_root, 1)

        @block.tensor
        def _(pe):
            def start(*name):
                b, n = place[name]
                if n > 1:
                    pe.wait_ge(read[b], n - 1)
                return bank[b]

            def done(ins, *name):
                ins.then_inc(full[place[name][0]], 1)

            def ada_row(g):
                pe.wait_ge(ada_summed, g + 1)
                b = start("ada", g)
                done(nc.tensor.matmul(b[:, :], ones, ada[:, g * HALF:(g + 1) * HALF], start=True, stop=True), "ada", g)

            def transposes(name, blocks):
                b = start(*name)
                for j, blk in enumerate(blocks):
                    ins = nc.tensor.transpose(b[:, j * P:(j + 1) * P], blk, ident[:, :])
                done(ins, *name)

            pe.wait_ge(made, 3)
            for g in range(4):
                ada_row(g)
            for t in range(NT):
                pe.wait_ge(h1_ready, t + 1)
                for s in range(2):
                    transposes(("h1T", t, s), [h1[:, t, (4 * s + j) * P:(4 * s + j + 1) * P] for j in range(4)])

            for g in ("zv", "v", "f", "zu"):
                if g == "f":
                    pe.wait_ge(fw_in, 16)
                    b = start("f")
                    for t in range(NT):
                        for k in range(KC):
                            ins = nc.tensor.matmul(b[:, t * HEADS:(t + 1) * HEADS], hT[:, k, t * P:(t + 1) * P],
                                                   f_w[:, k, :], start=(k == 0), stop=(k == KC - 1))
                    done(ins, "f")
                    continue
                w = wait_weights(pe, "w_in", g)
                for t in range(NT):
                    wait_read(pe, "h1T", t, 1)
                    wait_read(pe, "h1T", t, 0)
                    b = start(g, t)
                    for k in range(KC):
                        ins = nc.tensor.matmul(b[:, :], hT[:, k, t * P:(t + 1) * P], w[:, k, :],
                                               start=(k == 0), stop=(k == KC - 1))
                    done(ins, g, t)
            for g in ("q", "k"):
                w = wait_weights(pe, "w_in", g)
                for n in range(4):
                    b = start(g, n)
                    for k in range(KC):
                        ins = nc.tensor.matmul(b[:, :], w[:, k, n * P:(n + 1) * P], hT[:, k, :],
                                               start=(k == 0), stop=(k == KC - 1))
                    done(ins, g, n)
            for g in range(4, 12):
                ada_row(g)

            pe.wait_ge(f_done, 1)
            b = start("cum")
            for kt in range(NT):
                for st in range(kt + 1):
                    ins = nc.tensor.matmul(b[0:HEADS, kt * P:(kt + 1) * P], lsg[:, st * HEADS:(st + 1) * HEADS],
                                           tri if st == kt else ones, start=(st == 0), stop=(st == kt))
            done(ins, "cum")

            pe.wait_ge(sgw_masked, 1)
            pe.wait_ge(v_norm, 1)
            for n in range(4):
                b = start("sgu", n)
                for j in range(2):
                    h = 2 * n + j
                    ins = nc.tensor.matmul(b[:, j * 256:(j + 1) * 256].rearrange("p (t d) -> p t d", t=NT), sgw[:, h, :],
                                           y[:, :, HALF + h * DH:HALF + (h + 1) * DH], start=True, stop=True)
                done(ins, "sgu", n)

            def logits(n):
                qt, h = ATTN[n]
                keys = (qt + 1) * P
                b = start("S", n)
                nc.tensor.matmul(b[:, 0:keys], q_z[:, h, qt * P:(qt + 1) * P], kT[:, h // 2, 0:keys],
                                 start=True, stop=False)
                done(nc.tensor.matmul(b[:, 0:keys], ident[0:HEADS, h:h + 1].broadcast_to([HEADS, P]), ncum[:, 0:keys],
                                      start=False, stop=True), "S", n)

            def turn(n):
                qt, h = ATTN[n]
                wait_read(pe, "S", n)
                transposes(("PT", n), [p_exp[:, n % 2, kb * P:(kb + 1) * P] for kb in range(qt + 1)])

            def values(n):
                qt, h = ATTN[n]
                wait_read(pe, "PT", n)
                b = start("O", qt) if h == 0 else bank[place["O", qt][0]]
                for kb in range(qt + 1):
                    ins = nc.tensor.matmul(b[:, h * DH:(h + 1) * DH], p_T[:, n % 2, kb * P:(kb + 1) * P],
                                           v_tok[:, kb, h * DH:(h + 1) * DH], start=(kb == 0), stop=(kb == qt))
                if h == HEADS - 1:
                    done(ins, "O", qt)
                else:
                    ins.then_inc(pT_used, 1)

            wait_read(pe, "cum")
            wait_read(pe, "q", 3)
            wait_read(pe, "k", 3)
            wait_read(pe, "v", 3)
            for n in range(len(ATTN) + 2):
                if n < len(ATTN):
                    logits(n)
                if 1 <= n <= len(ATTN):
                    turn(n - 1)
                if n >= 2:
                    values(n - 2)

            def front(t):
                pe.wait_ge(y_ready, t + 1)
                for s in range(2):
                    transposes(("yT", t, s), [y[:, t, (4 * s + j) * P:(4 * s + j + 1) * P] for j in range(4)])
                pe.wait_ge(w_out_gated, 2 * KC)
                wait_read(pe, "yT", t, 0)
                wait_read(pe, "yT", t, 1)
                for s in range(2):
                    w = weights[:, slot_of["w_out", s], :, :]
                    b = start("mix", t, s)
                    for k in range(KC):
                        ins = nc.tensor.matmul(b[:, :], yT[:, k, :], w[:, k, :], start=(k == 0), stop=(k == KC - 1))
                    done(ins, "mix", t, s)
                pe.wait_ge(h2_ready, t + 1)
                for s in range(2):
                    transposes(("h2T", t, s), [y[:, t, (4 * s + j) * P:(4 * s + j + 1) * P] for j in range(4)])
                wait_read(pe, "h2T", t, 0)
                wait_read(pe, "h2T", t, 1)
                for g in range(4):
                    w = wait_weights(pe, "w_query", g)
                    b = start("qrow", t, g)
                    for k in range(KC):
                        ins = nc.tensor.matmul(b[:, :], h2T[:, k, :], w[:, k, :], start=(k == 0), stop=(k == KC - 1))
                    done(ins, "qrow", t, g)
                for g in range(4):
                    wait_read(pe, "qrow", t, g)
                    transposes(("qT", t, g), [qrow[:, (4 * g + j) * P:(4 * g + j + 1) * P] for j in range(4)])
                pe.wait_ge(keys_in, 16 * (t + 1))
                for g in range(4):
                    wait_read(pe, "qT", t, g)
                    b = start("score", t, g)
                    for j in range(4):
                        n = 4 * g + j
                        ins = nc.tensor.matmul(b[:, j * P:(j + 1) * P], qT[:, n, :], keysT[:, n, :], start=True, stop=True)
                    done(ins, "score", t, g)

            front(0)
            for t in range(NT):
                if t + 1 < NT:
                    front(t + 1)
                if t:
                    pe.wait_ge(acc_read, t)

                def weighted(i, first, last):
                    for n in range(DIAGS):
                        r = 2 * n
                        pe.wait_ge(diag_ready, t * V_PE + DIAGS * i + n + 1)
                        pe.wait_ge(gathered[r], 16 * ((2 * t + 1) * ROUNDS + i + 1))
                        for s in range(2):
                            ins = nc.tensor.matmul(bank[6 + s][:, :], diag[:, n, :],
                                                   ring[:, r, s * HALF:(s + 1) * HALF],
                                                   start=(first and n == 0), stop=(last and n == DIAGS - 1))
                        ins.then_inc(v_used, 1)

                weighted(0, True, False)
                with pe.Fori(1, ROUNDS - 1) as i:
                    weighted(i, False, False)
                weighted(ROUNDS - 1, False, True)

        @block.vector
        def _(dve):
            links = [0]

            def link(ins):
                links[0] += 1
                ins.then_inc(v_chain, 1)
                dve.wait_ge(v_chain, links[0])

            tt, ts, stt = nc.vector.tensor_tensor, nc.vector.tensor_scalar, nc.vector.scalar_tensor_tensor

            dve.wait_ge(c_exped, 1)
            link(ts(c_exp, c_exp, 1.0, None, ALU.add))
            link(nc.vector.reciprocal(c_exp, c_exp))
            link(tt(c_act, c_col, c_exp, ALU.mult))

            def ada_sum(g):
                w = wait_weights(dve, "ada", g)
                acc = ada[:, g * HALF:(g + 1) * HALF]
                for k in range(KC):
                    ins = stt(out=acc, in0=w[:, k, :], scalar=c_act[:, k:k + 1], in1=acc, op0=ALU.mult, op1=ALU.add)
                    if k < KC - 1:
                        link(ins)
                ins.then_inc(ada_summed, 1)

            dve.wait_ge(b_ada_in, 16)
            for g in range(4):
                ada_sum(g)
            dve.wait_ge(x_squared, NT)
            ts(x_ss, x_ss, 1.0 / D, EPS, ALU.mult, ALU.add).then_inc(x_mean, 1)
            dve.wait_ge(x_root, 1)
            link(nc.vector.reciprocal(x_rms, x_rms))
            dve.wait_ge(made, 3)
            link(nc.vector.tensor_copy(iota16, iota_u))
            for g in range(4):
                wait_read(dve, "ada", g)
            dve.wait_ge(norm1_in, 16)
            stt(out=scale1, in0=scale1, scalar=1.0, in1=norm1_row, op0=ALU.add, op1=ALU.mult).then_inc(a1_done, 1)
            dve.wait_ge(a1_done, 1)
            for t in range(NT):
                link(stt(out=h1[:, t, :], in0=xs[:, t, :], scalar=x_rms[:, t:t + 1], in1=scale1, op0=ALU.mult, op1=ALU.mult))
                tt(h1[:, t, :], h1[:, t, :], shift1, ALU.add).then_inc(h1_ready, 1)
            for t in range(NT):
                b = wait_full(dve, "v", t)
                release(nc.vector.tensor_copy(v_tok[:, t, :], b[:, :]), "v", t)

            b = wait_full(dve, "f")
            dve.wait_ge(small_in, 48)
            ins = tt(logit.rearrange("p (t h) -> p t h", t=NT), b[:, 0:32].rearrange("p (t h) -> p t h", t=NT),
                     bf_row.unsqueeze(1).broadcast_to([P, NT, HEADS]), ALU.add)
            release(ins, "f")
            wait_read(dve, "f")
            stt(out=lsg_e, in0=logit, scalar=-1.0, in1=logit, op0=ALU.mult, op1=ALU.max).then_inc(f_abs, 1)
            dve.wait_ge(f_exp, 1)
            ts(lsg_e, lsg_e, 1.0, None, ALU.add).then_inc(f_plus, 1)
            dve.wait_ge(f_log, 1)
            stt(out=lsg, in0=logit, scalar=0.0, in1=lsg_e, op0=ALU.min, op1=ALU.subtract).then_inc(f_done, 1)

            zv = y[:, :, HALF:D].rearrange("p t (h d) -> p t h d", h=HEADS)

            def per_head(s):
                return s.rearrange("p (t h) -> p t h", t=NT)

            def over_head(s):
                return per_head(s).unsqueeze(3).broadcast_to([P, NT, HEADS, DH])

            wait_read(dve, "zv", NT - 1)
            link(nc.vector.tensor_reduce(per_head(v_mean), zv, AX_X, ALU.add))
            link(ts(v_mean, v_mean, -1.0 / DH, None, ALU.mult))
            for t in range(NT):
                ins = tt(zv[:, t], zv[:, t], per_head(v_mean)[:, t].unsqueeze(2).broadcast_to([P, HEADS, DH]), ALU.add)
            link(ins)
            sq = v_sq.rearrange("p (t d) -> p t d", t=2)
            for n in range(2):
                link(tt(sq, y[:, 2 * n:2 * n + 2, HALF:D], y[:, 2 * n:2 * n + 2, HALF:D], ALU.mult))
                link(nc.vector.tensor_reduce(v_var[:, 16 * n:16 * n + 16], v_sq.rearrange("p (g d) -> p g d", d=DH), AX_X, ALU.add))
            ts(v_var, v_var, 1.0 / DH, EPS, ALU.mult, ALU.add).then_inc(v_var_ready, 1)
            for g in range(4, 7):
                ada_sum(g)
            for n in range(4):
                b = wait_full(dve, "k", n)
                release(nc.vector.tensor_copy(kT[:, n, :], b[:, :]), "k", n)
            dve.wait_ge(v_root, 1)
            link(nc.vector.reciprocal(v_var, v_var))
            for t in range(NT):
                ins = tt(zv[:, t], zv[:, t], per_head(v_var)[:, t].unsqueeze(2).broadcast_to([P, HEADS, DH]), ALU.mult)
            link(ins)
            dve.wait_ge(ln_in, 32)
            zvf = y[:, :, HALF:D]
            link(tt(zvf, zvf, ln_g.unsqueeze(1).broadcast_to([P, NT, HALF]), ALU.mult))
            tt(zvf, zvf, ln_b.unsqueeze(1).broadcast_to([P, NT, HALF]), ALU.add).then_inc(v_norm, 1)
            for g in range(7, 12):
                ada_sum(g)
            for g in range(8, 10):
                wait_read(dve, "ada", g)
            dve.wait_ge(norm2_in, 16)
            stt(out=scale2, in0=scale2, scalar=1.0, in1=norm2_row, op0=ALU.add, op1=ALU.mult).then_inc(a2_done, 1)

            wait_read(dve, "zu", NT - 1)
            for n in range(4):
                b = wait_full(dve, "sgu", n)
                for j in range(2):
                    h = 2 * n + j
                    zu = y[:, :, h * DH:(h + 1) * DH]
                    ins = stt(out=zu, in0=b[:, j * 256:(j + 1) * 256].rearrange("p (t d) -> p t d", t=NT),
                              scalar=sgb[:, h:h + 1], in1=zu, op0=ALU.add, op1=ALU.mult)
                release(ins, "sgu", n)

            def row_max(n):
                qt, h = ATTN[n]
                keys = (qt + 1) * P
                b = wait_full(dve, "S", n)
                own = b[:, qt * P:keys]
                link(tt(own, own, causal, ALU.add))
                nc.vector.tensor_reduce(nmax[:, n:n + 1], b[:, 0:keys], AX_X, ALU.max, negate=True).then_inc(neg_max, 1)

            def copy_turned(n):
                qt, h = ATTN[n]
                b = wait_full(dve, "PT", n)
                if n >= 2:
                    was_qt, was_h = ATTN[n - 2]
                    if was_h == HEADS - 1:
                        wait_full(dve, "O", was_qt)
                    else:
                        dve.wait_ge(pT_used, was_qt * (HEADS - 1) + was_h + 1)
                release(nc.vector.tensor_copy(p_T[:, n % 2, 0:(qt + 1) * P], b[:, 0:(qt + 1) * P]), "PT", n)

            def output(qt):
                b = wait_full(dve, "O", qt)
                rs = slice(qt * HEADS, (qt + 1) * HEADS)
                for n in (-2, -1):
                    wait_read(dve, "S", (qt + 1) * HEADS + n)
                link(nc.vector.reciprocal(o_scale[:, rs], rsum[:, rs]))
                release(tt(y[:, qt, HALF:D].rearrange("p (h d) -> p h d", h=HEADS),
                           b[:, :].rearrange("p (h d) -> p h d", h=HEADS),
                           o_scale[:, rs].unsqueeze(2).broadcast_to([P, HEADS, DH]), ALU.mult), "O", qt)

            dve.wait_ge(causal_made, 1)
            for n in range(len(ATTN) + 2):
                if n < len(ATTN):
                    row_max(n)
                if 1 <= n <= len(ATTN):
                    copy_turned(n - 1)
                if n >= 2 and ATTN[n - 2][1] == HEADS - 1:
                    output(ATTN[n - 2][0])

            def head_mean(t):
                dve.wait_ge(y_squared, t + 1)
                link(nc.vector.tensor_reduce(y_var, squares.rearrange("p (h d) -> p h d", d=DH), AX_X, ALU.add))
                ts(y_var, y_var, 1.0 / DH, EPS, ALU.mult, ALU.add).then_inc(y_mean, 1)

            def head_norm(t):
                dve.wait_ge(y_root, t + 1)
                link(nc.vector.reciprocal(y_rms, y_rms))
                yh = y[:, t, :].rearrange("p (h d) -> p h d", d=DH)
                tt(yh, yh, y_rms.unsqueeze(2).broadcast_to([P, 2 * HEADS, DH]), ALU.mult).then_inc(y_ready, 1)

            def turned_y(t):
                for s in range(2):
                    b = wait_full(dve, "yT", t, s)
                    release(tt(yT[:, 4 * s:4 * s + 4, :], b[:, :].rearrange("p (k t) -> p k t", k=4),
                               out_g[:, 4 * s:4 * s + 4].unsqueeze(2).broadcast_to([P, 4, P]), ALU.mult), "yT", t, s)

            def residual(t):
                for s in range(2):
                    b = wait_full(dve, "mix", t, s)
                    xh = xs[:, t, s * HALF:(s + 1) * HALF]
                    release(tt(xh, b[:, :], xh, ALU.add), "mix", t, s)

            def x1_stat(t):
                dve.wait_ge(x1_squared, t + 1)
                ts(x1_ss, x1_ss, 1.0 / D, EPS, ALU.mult, ALU.add).then_inc(x1_mean, 1)

            def second_norm(t):
                dve.wait_ge(x1_root, t + 1)
                link(nc.vector.reciprocal(x1_rms, x1_rms))
                link(stt(out=y[:, t, :], in0=xs[:, t, :], scalar=x1_rms, in1=scale2, op0=ALU.mult, op1=ALU.mult))
                tt(y[:, t, :], y[:, t, :], shift2, ALU.add).then_inc(h2_ready, 1)

            pieces = [head_mean, head_norm, turned_y, residual, x1_stat, second_norm]

            def top16(values_out, index_out, rows, groups):
                for g in range(groups):
                    ins = nc.vector.max(values_out[:, g, 0:8], rows[:, g, :])
                link(ins)
                for g in range(groups):
                    ins = nc.vector.max_index(index_out[:, g, 0:8], values_out[:, g, 0:8], rows[:, g, :])
                link(ins)
                yield
                for g in range(groups):
                    ins = nc.vector.match_replace(rows[:, g, :], values_out[:, g, 0:8], rows[:, g, :], TAKEN)
                link(ins)
                yield
                for g in range(groups):
                    ins = nc.vector.max(values_out[:, g, 8:16], rows[:, g, :])
                link(ins)
                for g in range(groups):
                    ins = nc.vector.max_index(index_out[:, g, 8:16], values_out[:, g, 8:16], rows[:, g, :])
                link(ins)

            def retrieve(t):
                for g in range(4):
                    wait_read(dve, "score", t, g)
                yield from top16(top_v, top_i, scores, HP)
                yield
                halves_v = top_v.rearrange("p (h s) k -> p h s k", s=2)
                link(tt(cand.rearrange("p h (a b) -> p h a b", b=TOPK),
                        halves_v[:, :, 0, :].unsqueeze(3).broadcast_to([P, PH, TOPK, TOPK]),
                        halves_v[:, :, 1, :].unsqueeze(2).broadcast_to([P, PH, TOPK, TOPK]), ALU.add))
                yield from top16(best_v, best_p, cand, PH)
                yield
                tt(gate[:, :].rearrange("p (h k) -> p h k", h=PH), best_v,
                   best_v[:, :, 0:1].broadcast_to([P, PH, TOPK]), ALU.subtract).then_inc(best_ready, 1)
                link(nc.vector.tensor_copy(top_f, top_i))
                flat_p = best_p.rearrange("p h k -> p (h k)")
                half_f = top_f.rearrange("p (h s) k -> p h s k", s=2)
                for s, place_f, picked in ((0, pos_a, sel_i), (1, pos_b, sel_j)):
                    if s == 0:
                        link(ts(pos_u, flat_p, 4, None, ALU.logical_shift_right))
                    else:
                        link(ts(pos_u, flat_p, 15, None, ALU.bitwise_and))
                    link(nc.vector.tensor_copy(place_f, pos_u))
                    for hh in range(2):
                        sel = slice(64 * hh, 64 * hh + 64)
                        link(tt(onehot, place_f[:, sel].unsqueeze(2).broadcast_to([P, 64, TOPK]),
                                iota16.unsqueeze(1).broadcast_to([P, 64, TOPK]), ALU.is_equal))
                        oh = onehot.rearrange("p (h k) a -> p h k a", h=4)
                        link(tt(oh, oh, half_f[:, 4 * hh:4 * hh + 4, s, :].unsqueeze(2).broadcast_to([P, 4, TOPK, TOPK]),
                                ALU.mult))
                        link(nc.vector.tensor_reduce(picked[:, sel], onehot, AX_X, ALU.add))
                    if s == 0:
                        yield
                stt(out=idx[:, t % 2, :], in0=sel_i, scalar=float(NKEYS), in1=sel_j, op0=ALU.mult, op1=ALU.add)\
                    .then_inc(topk_done, 1)

            def gates(t):
                dve.wait_ge(gate_exp, t + 1)
                gh = gate[:, :].rearrange("p (h k) -> p h k", h=PH)
                link(nc.vector.tensor_reduce(gate_sum, gh, AX_X, ALU.add))
                link(nc.vector.reciprocal(gate_sum, gate_sum))
                link(tt(gh, gh, gate_sum.unsqueeze(2).broadcast_to([P, PH, TOPK]), ALU.mult))

            for piece in pieces:
                piece(0)
            for _step in retrieve(0):
                pass
            gates(0)
            for t in range(NT):
                def dots(first, last):
                    with dve.Fori(first, last) as i:
                        for r in range(RING):
                            dve.wait_ge(gathered[r], 16 * (2 * t * ROUNDS + i + 1))
                            stt(out=ring[:, r, :], in0=ring[:, r, :], scalar=1.0, in1=y[:, t, :], op0=ALU.mult, op1=ALU.mult,
                                accum_out=act_w[:, bass.ds(RING * i + r, 1)]).then_inc(dot_done, 1)

                if t + 1 < NT:
                    for n, piece in enumerate(pieces):
                        dots(2 * n, 2 * n + 2)
                        piece(t + 1)
                    dots(2 * len(pieces), ROUNDS)
                else:
                    dots(0, ROUNDS)
                dve.wait_ge(gelu_done, t + 1)
                tt(act_w[:, :], act_w[:, :], gate[:, :], ALU.mult).then_inc(w_ready, 1)
                dve.wait_ge(w_ready, t + 1)
                dve.wait_ge(dot_done, (t + 1) * NSEL)

                def weighted(i, first):
                    for n in range(DIAGS):
                        r = 2 * n + 1
                        dve.wait_ge(gathered[r], 16 * ((2 * t + 1) * ROUNDS + i + 1))
                        w = act_w[:, bass.ds(RING * i + r, 1)]
                        if first and n == 0:
                            ins = ts(y[:, t, :], ring[:, r, :], w, None, ALU.mult)
                        else:
                            dve.wait_ge(v_added, t * V_PE + DIAGS * i + n)
                            ins = stt(out=y[:, t, :], in0=ring[:, r, :], scalar=w, in1=y[:, t, :], op0=ALU.mult, op1=ALU.add)
                        ins.then_inc(v_added, 1)

                weighted(0, True)
                steps = retrieve(t + 1) if t + 1 < NT else iter(())
                done = 1
                for _step in steps:
                    with dve.Fori(done, done + 1) as i:
                        weighted(i, False)
                    done += 1
                with dve.Fori(done, ROUNDS) as i:
                    weighted(i, False)
                if t + 1 < NT:
                    gates(t + 1)
                dve.wait_ge(v_used, (t + 1) * V_PE)
                dve.wait_ge(v_added, (t + 1) * V_PE)
                for s in range(2):
                    cols = slice(s * HALF, (s + 1) * HALF)
                    ins = tt(y[:, t, cols], bank[6 + s][:, :], y[:, t, cols], ALU.add)
                ins.then_inc(acc_read, 1)
                dve.wait_ge(acc_read, t + 1)
                link(tt(y[:, t, :], y[:, t, :], gate2, ALU.mult))
                tt(xs[:, t, :], xs[:, t, :], y[:, t, :], ALU.add).then_inc(x2_ready, 1)
                dve.wait_ge(x2_squared, t + 1)
                ts(x2_ss, x2_ss, 1.0 / D, EPS, ALU.mult, ALU.add).then_inc(x2_mean, 1)
                dve.wait_ge(x2_root, t + 1)
                link(nc.vector.reciprocal(x2_rms, x2_rms))
                dve.wait_ge(final_in, 16)
                stt(out=xs[:, t, :], in0=xs[:, t, :], scalar=x2_rms, in1=final_row[:, :], op0=ALU.mult, op1=ALU.mult)\
                    .then_inc(out_ready, 1)


def kernel(x, c, w_ada, b_ada, norm1_g, w_in, b_f, sg_ln_g, sg_ln_b, sg_w, sg_b, out_g_sg, out_g_fox,
           w_out, norm2_g, w_query, sub_keys, expert_u, expert_v, final_g):
    import concourse.bacc as bacc
    import numpy as np
    from concourse.bass_utils import run_bass_kernel_spmd

    laid_out = {
        "x": x[0], "cT": np.transpose(c.reshape(KC, P)), "w_ada": w_ada[0], "b_ada": b_ada[0], "norm1_g": norm1_g[0], "w_in": w_in[0],
        "b_f": b_f[0], "sg_ln_g": sg_ln_g[0], "sg_ln_b": sg_ln_b[0],
        "sg_wT": np.transpose(sg_w[0], (2, 0, 1)),
        "sg_bT": np.transpose(sg_b[0]),
        "out_gT": np.transpose(np.concatenate([out_g_sg[0], out_g_fox[0]]).reshape(KC, P)), "w_out": w_out[0], "norm2_g": norm2_g[0],
        "w_query": w_query[0],
        "sub_keysT": np.transpose(sub_keys[0].reshape(HP, NKEYS, P), (2, 0, 1)),
        "expert_u": expert_u[0], "expert_v": expert_v[0], "final_g": final_g,
    }
    nc = bacc.Bacc("TRN2", target_bir_lowering=False, num_devices=1)
    arrays, args = {}, []
    for name, a in laid_out.items():
        a = np.ascontiguousarray(a)
        arrays[f"in_{name}"] = a
        args.append(nc.dram_tensor(f"in_{name}", a.shape, mybir.dt.from_np(a.dtype), kind="ExternalInput").ap())
    args.append(nc.dram_tensor("out", (SEQ, D), F32, kind="ExternalOutput").ap())
    program(nc, *args)
    result = run_bass_kernel_spmd(nc, [arrays], core_ids=[0])
    return result.results[0]["out"].reshape(1, SEQ, D)
```

```python
from contextlib import ExitStack

import concourse.bass as bass
from concourse import mybir

F32 = mybir.dt.float32
F32R = mybir.dt.float32r
U32 = mybir.dt.uint32
ALU = mybir.AluOpType
ACT = mybir.ActivationFunctionType
AX_X = mybir.AxisListType.X

P = 128
SEQ = 512
D = 1024
NT = SEQ // P
KC = D // P
HALF = 512
HEADS = 8
DH = 64
PH = 8
HP = 2 * PH
NKEYS = 128
TOPK = 16
NSEL = PH * TOPK
N_EXPERTS = NKEYS * NKEYS
EPS = 1e-6
MASKED = -1e30
TAKEN = -3e38

SPARSE = 0
ORDER = (1, 2, 3, SPARSE)
DENSE = NT - 1
DTOK = DENSE * P
ROWS = 4
STEP_ROWS = 2
STAGED = 8
GROUP = 32
GROUPS = DTOK // GROUP
BATCH = 4
BATCHES = P // BATCH
AHEAD = 8
BODY = 8
ITERS = NKEYS // BODY
GLOAD = 4
SLOTS = 6
ADA_EARLY = [("ada", g) for g in range(4)]
W_IN = [("w_in", c) for c in ("zv", "v", "zu", "q", "k")]
ADA_LATE = [("ada", g) for g in range(4, 12)]
RESIDENT = [("w_query", 0), ("w_out", 0), ("w_out", 1)] + [("w_query", g) for g in range(1, 4)]
STREAM = ADA_EARLY + W_IN + ADA_LATE + RESIDENT
W_IN_COL = {"zu": 0, "zv": 512, "q": 1024, "k": 1536, "v": 2048}
F_COL = 2560

ATTN = [(qt, h) for qt in range(NT) for h in range(HEADS)]


def plan_banks():
    jobs = [(("ada", g), 4 + g % 2) for g in range(4)]
    jobs += [(("h1T", t, s), 6 + s) for t in range(NT) for s in range(2)]
    proj = [("zv", t) for t in range(NT)] + [("v", t) for t in range(NT)] + [("f",)]
    proj += [("zu", t) for t in range(NT)] + [("q", c) for c in range(4)] + [("k", c) for c in range(4)]
    jobs += [(j, n % 4) for n, j in enumerate(proj)]
    jobs += [(("ada", g), 4 + g % 2) for g in range(4, 12)]
    jobs += [(("cum",), 6)]
    jobs += [(("sgu", b), b) for b in range(4)]
    jobs += [(("S", n), 4 + n % 2) for n in range(len(ATTN))]
    jobs += [(("PT", n), 6 + n % 2) for n in range(len(ATTN))]
    jobs += [(("O", t), t % 2) for t in range(NT)]
    jobs += [(("yT", t, s), (2, 6)[t % 2] + s) for t in range(NT) for s in range(2)]
    jobs += [(("mix", t, s), (0, 4)[t % 2] + s) for t in range(NT) for s in range(2)]
    jobs += [(("h2T", t, s), (2, 6)[t % 2] + s) for t in range(NT) for s in range(2)]
    for n in range(NT):
        jobs += [(("qrow", n, g), (4, 5, 0, 1)[g]) for g in range(4)]
        jobs += [(("qT", n, g), (2, 3, 4, 5)[g]) for g in range(4)]
        jobs += [(("score", n, g), g) for g in range(4)]
        if 1 <= n < NT:
            jobs += [(("turn", n - 1), 6)]
    place, count = {}, [0] * 8
    for name, b in jobs:
        count[b] += 1
        place[name] = (b, count[b])
    return place


def program(nc, x, cT, w_ada, b_ada, norm1_g, w_in, b_f, sg_ln_g, sg_ln_b, sg_wT, sg_bT,
            out_gT, w_out, norm2_g, w_query, sub_keysT, uT, expert_u, expert_v, final_g, out):
    place = plan_banks()
    slot_of = {name: n % SLOTS for n, name in enumerate(STREAM)}
    load_of = {name: 16 * (n // SLOTS + 1) for n, name in enumerate(STREAM)}

    with ExitStack() as ctx:
        def sb(name, shape, dt=F32):
            return ctx.enter_context(nc.sbuf_tensor(name, shape, dt))

        def sem(name):
            return ctx.enter_context(nc.semaphore(name))

        def aligned(offset):
            return (offset + 31) // 32 * 32

        weights_at = aligned(nc.sbuf_base)
        weights = sb("weights", [P, SLOTS, KC, HALF])
        shared_at = aligned(nc.sbuf_base)
        shared = sb("shared", [P, 8 * D])
        xs = sb("xs", [P, NT, D])
        ada = sb("ada", [P, 6 * D])
        hT = sb("hT", [P, KC, SEQ])
        y_at = aligned(nc.sbuf_base)
        y = sb("y", [P, NT, D])
        ident = sb("ident", [P, P])
        final_row = sb("final_row", [P, D])
        idx = sb("idx", [P, 2, NSEL], U32)
        gate = sb("gate", [P, NSEL])
        act_w = sb("act_w", [P, NSEL])
        misc = sb("misc", [P, 160])
        idx_slot = sb("idx_slot", [P, 2, STAGED], U32)

        h1 = shared[:, 0:4 * D].rearrange("p (t d) -> p t d", t=NT)
        q_z = shared[:, 0:4 * D].rearrange("p (h s) -> p h s", h=HEADS)
        kT = shared[:, 4 * D:6 * D].rearrange("p (c s) -> p c s", c=4)
        v_tok = shared[:, 6 * D:8 * D].rearrange("p (t d) -> p t d", t=NT)

        hTf = hT[:, :, :].rearrange("p k s -> p (k s)")
        norm1_row = hTf[:, 0:D]
        sgw = hTf[:, 0:D].rearrange("p (h t) -> p h t", h=HEADS)
        p_exp = hTf[:, D:2 * D].rearrange("p (b s) -> p b s", b=2)
        p_T = hTf[:, 2 * D:3 * D].rearrange("p (b s) -> p b s", b=2)
        ncum = hTf[0:HEADS, 3 * D:3 * D + SEQ]
        causal = hTf[:, 3 * D + SEQ:3 * D + SEQ + P]
        squares = shared[:, 0:4 * D].rearrange("p (t d) -> p t d", t=NT)
        yT = shared[:, 4 * D:8 * D].rearrange("p (t k n) -> p t k n", t=NT, k=KC)
        h2T_sparse = shared[:, 4 * D:5 * D].rearrange("p (k t) -> p k t", k=KC)
        ring = hTf.rearrange("p (r d) -> p r d", r=ROWS)

        def h2T(t):
            return h2T_sparse if t == SPARSE else y[:, t, :].rearrange("p (k t) -> p k t", k=KC)

        def scratch(n):
            return (shared, hTf)[n % 2]

        def qT(n):
            return scratch(n)[:, 0:2 * D].rearrange("p (g t) -> p g t", g=HP)

        def cand_of(n):
            return scratch(n)[:, 0:2 * D].rearrange("p (h e) -> p h e", h=PH)

        def qrow(n):
            return scratch(n)[:, 2 * D:4 * D]

        def scores(n):
            return scratch(n)[:, 2 * D:4 * D].rearrange("p (g n) -> p g n", g=HP)

        def picks(n):
            return [scratch(n)[:, 2 * D + j * NSEL:2 * D + (j + 1) * NSEL] for j in range(5)]

        hot_j = shared[:, 5 * D:6 * D].rearrange("p (b t j) -> p b t j", b=2, t=BATCH)
        hot_i = shared[:, 6 * D:7 * D].rearrange("p (b t i) -> p b t i", b=2, t=BATCH)

        def slot(n):
            return weights[:, n, :, :].rearrange("p k n -> p (k n)")

        def slot_f32r(name, n, first, shape):
            return nc.alloc_sbuf_tensor_at(name, shape, F32R, offset=weights_at + 4 * (n * KC * HALF + first))

        staging = [slot(b).rearrange("p (i t) -> p i t", t=GROUP) for b in range(2)]
        u_raw = slot(2)[:, 0:2 * D].rearrange("p (b n) -> p b n", b=2)
        u_lo = slot_f32r("u_lo", 2, 0, [P, 2, D])
        u_hi = slot_f32r("u_hi", 2, 2 * D, [P, 2, D])
        ahead = slot(3)[:, 0:AHEAD * DTOK].rearrange("p (b n) -> p b n", b=AHEAD)
        v_raw = slot(4)[:, 0:2 * D].rearrange("p (b n) -> p b n", b=2)
        v_lo = slot_f32r("v_lo", 4, 0, [P, 2, D])
        v_hi = slot_f32r("v_hi", 4, 2 * D, [P, 2, D])
        g_block = slot(5)[:, 0:2 * GLOAD * DTOK].rearrange("p (b g i t) -> p b g i t", b=2, g=GROUPS, i=GLOAD)
        w_raw = slot(0)[:, 0:2 * DTOK].rearrange("p (b n) -> p b n", b=2)
        w_lo = slot_f32r("w_lo", 0, 0, [P, 2, DTOK])
        w_hi = slot_f32r("w_hi", 0, 2 * DTOK, [P, 2, DTOK])
        h2_hi = nc.alloc_sbuf_tensor_at("h2_hi", [P, DENSE, KC, P], F32R, offset=shared_at)
        h2_lo = nc.alloc_sbuf_tensor_at("h2_lo", [P, DENSE, KC, P], F32R, offset=y_at + 4 * D)
        g_dram = nc.dram_tensor("gates_dense", (GROUPS, P, NKEYS * GROUP), F32).ap()

        def row(n):
            return ada[:, n * D:(n + 1) * D]
        shift1, scale1, gate1, shift2, scale2, gate2 = (row(n) for n in range(6))
        ln_g, ln_b = ada[:, 0:HALF], ada[:, HALF:D]
        v_sq = ada[:, D:2 * D]
        norm2_row = ada[:, D:2 * D]
        keysT = ada[:, 0:2 * D].rearrange("p (g n) -> p g n", g=HP)
        onehot = row(3).rearrange("p (s a) -> p s a", a=TOPK)
        top_v = row(4)[:, 0:256].rearrange("p (g k) -> p g k", g=HP)
        top_i = row(4)[:, 256:512].bitcast(U32).rearrange("p (g k) -> p g k", g=HP)
        top_f = row(4)[:, 512:768].rearrange("p (g k) -> p g k", g=HP)
        best_v = row(4)[:, 768:896].rearrange("p (h k) -> p h k", h=PH)
        best_p = row(4)[:, 896:1024].bitcast(U32).rearrange("p (h k) -> p h k", h=PH)
        turned = ada[:, 2 * D:2 * D + 6 * P].rearrange("p (b c t) -> p b c t", b=2, c=3)
        iota128 = ada[:, 2 * D + 6 * P:2 * D + 7 * P]

        tri = act_w[:, :]
        c_col, c_act, c_exp = misc[:, 0:8], misc[:, 8:16], misc[:, 16:24]
        out_g = misc[:, 24:32]
        sgb = misc[:, 32:40]
        bf_row = misc[:, 40:48]
        iota16 = misc[:, 48:64]
        x_ss, x_rms = misc[:, 64:68], misc[:, 68:72]
        y_var = act_w[:, 0:64].rearrange("p (t h) -> p t h", t=NT)
        y_rms = act_w[:, 64:128].rearrange("p (t h) -> p t h", t=NT)
        j_now = misc[:, 128:128 + 2 * BATCH].rearrange("p (b t) -> p b t", b=2)
        x1_ss, x1_rms = misc[:, 104:108], misc[:, 116:120]
        x2_ss, x2_rms = misc[:, 120:124], misc[:, 124:128]
        gate_sum = misc[:, 108:116]
        logit = idx[:, 0, 0:32].bitcast(F32)
        lsg_e = idx[:, 0, 32:64].bitcast(F32)
        lsg = idx[:, 0, 64:96].bitcast(F32)
        nmax = idx[:, 0, 96:128].bitcast(F32)
        rsum = idx[:, 1, 0:32].bitcast(F32)
        v_mean = idx[:, 1, 32:64].bitcast(F32)
        v_var = idx[:, 1, 64:96].bitcast(F32)
        o_scale = idx[:, 1, 96:128].bitcast(F32)
        f_w = gate[:, 0:64].rearrange("p (k f) -> p k f", k=KC)
        iota128_u = idx[:, 1, :]
        iota_u = gate[:, 64:80].bitcast(U32)
        ones = gate[:, 80:81].broadcast_to([P, P])

        bank = [ctx.enter_context(nc.psum_tensor(f"bank{b}", [P, HALF], F32)) for b in range(8)]

        weight_in = [sem(f"weight_in{s}") for s in range(SLOTS)]
        full = [sem(f"bank{b}_full") for b in range(8)]
        read = [sem(f"bank{b}_read") for b in range(8)]
        gathered = [sem(f"gathered{r}") for r in range(ROWS)]
        g_stored = [sem(f"g_stored{b}") for b in range(2)]
        g_in = [sem(f"g_in{b}") for b in range(2)]
        u_in = [sem(f"u_in{b}") for b in range(2)]
        v_in = [sem(f"v_in{b}") for b in range(2)]
        x_in, c_in, small_in, norm1_in = sem("x_in"), sem("c_in"), sem("small_in"), sem("norm1_in")
        b_ada_in, norm2_in, ln_in, sgw_in = sem("b_ada_in"), sem("norm2_in"), sem("ln_in"), sem("sgw_in")
        final_in, fw_in, keys_in, stored = sem("final_in"), sem("fw_in"), sem("keys_in"), sem("stored")
        made, causal_made, sgw_masked, qz_zero = sem("made"), sem("causal_made"), sem("sgw_masked"), sem("qz_zero")
        c_exped = sem("c_exped")
        ada_summed = sem("ada_summed")
        a1_done, a2_done, h1_ready = sem("a1_done"), sem("a2_done"), sem("h1_ready")
        x_squared, x_mean, x_root = sem("x_squared"), sem("x_mean"), sem("x_root")
        f_abs, f_exp, f_plus, f_log, f_done = sem("f_abs"), sem("f_exp"), sem("f_plus"), sem("f_log"), sem("f_done")
        v_var_ready, v_root, v_norm = sem("v_var_ready"), sem("v_root"), sem("v_norm")
        neg_max, pT_used = sem("neg_max"), sem("pT_used")
        w_out_gated = sem("w_out_gated")
        y_squared, y_mean, y_root, y_ready = sem("y_squared"), sem("y_mean"), sem("y_root"), sem("y_ready")
        x1_squared, x1_mean, x1_root, h2_ready = sem("x1_squared"), sem("x1_mean"), sem("x1_root"), sem("h2_ready")
        best_ready, gate_exp, topk_done = sem("best_ready"), sem("gate_exp"), sem("topk_done")
        granted, idx_staged = sem("slot_granted"), sem("idx_staged")
        dot_done, gelu_done, w_ready = sem("dot_done"), sem("gelu_done"), sem("w_ready")
        v_added = sem("v_added")
        j_staged, hot_granted = sem("j_staged"), sem("hot_granted")
        gates_ready, iota_made = sem("gates_ready"), sem("iota_made")
        hot_j_made, hot_i_made, built = sem("hot_j_made"), sem("hot_i_made"), sem("built")
        build_granted, build_read = sem("build_granted"), sem("build_read")
        h2_hi_made, h2_lo_made = sem("h2_hi_made"), sem("h2_lo_made")
        u_hi_made, u_lo_made, v_hi_made, v_lo_made = sem("u_hi_made"), sem("u_lo_made"), sem("v_hi_made"), sem("v_lo_made")
        w_made, w_hi_made, w_lo_made = sem("w_made"), sem("w_hi_made"), sem("w_lo_made")
        a_full, a_read = sem("a_full"), sem("a_read")
        v_used = sem("v_used")
        x2_ready, x2_squared, x2_mean, x2_root = sem("x2_ready"), sem("x2_squared"), sem("x2_mean"), sem("x2_root")
        out_ready = sem("out_ready")
        v_chain, g_chain = sem("vector_chain"), sem("gpsimd_chain")

        block = ctx.enter_context(nc.Block())

        def wait_full(eng, *name):
            b, n = place[name]
            eng.wait_ge(full[b], n)
            return bank[b]

        def wait_read(eng, *name):
            b, n = place[name]
            eng.wait_ge(read[b], n)

        def release(ins, *name):
            ins.then_inc(read[place[name][0]], 1)

        def group_source(kind, g):
            if kind == "ada":
                src = w_ada[:, g * HALF:(g + 1) * HALF]
            elif kind == "w_in":
                src = w_in[:, W_IN_COL[g]:W_IN_COL[g] + HALF]
            elif kind == "w_out":
                src = w_out[:, g * HALF:(g + 1) * HALF]
            else:
                src = w_query[:, g * HALF:(g + 1) * HALF]
            return src.rearrange("(k p) n -> p k n", p=P)

        def one_row(v):
            return v.rearrange("(a n) -> a n", a=1)

        def on_all(v):
            return one_row(v).broadcast_to([P, v.shape[0]])

        def wait_weights(eng, *name):
            eng.wait_ge(weight_in[slot_of[name]], load_of[name])
            return weights[:, slot_of[name], :, :]

        @block.sync
        def _(sp):
            def load_group(n):
                name = STREAM[n]
                if n >= SLOTS:
                    kind, g = STREAM[n - SLOTS]
                    if kind == "ada":
                        sp.wait_ge(ada_summed, g + 1)
                    else:
                        wait_full(sp, g, 3)
                sp.dma_start(weights[:, slot_of[name], :, :], group_source(*name)).then_inc(weight_in[slot_of[name]], 16)

            sp.dma_start(c_col, cT).then_inc(c_in, 16)
            load_group(0)
            sp.dma_start(xs[:, :, :], x.rearrange("(t p) d -> p t d", p=P)).then_inc(x_in, 16)
            for n in range(1, 4):
                load_group(n)
            sp.dma_start(norm1_row, on_all(norm1_g)).then_inc(norm1_in, 16)
            for n in range(4, SLOTS):
                load_group(n)
            sp.wait_ge(made, 3)
            sp.dma_start(f_w, w_in[:, F_COL:F_COL + HEADS].rearrange("(k p) n -> p k n", p=P)).then_inc(fw_in, 16)
            sp.dma_start(bf_row, on_all(b_f)).then_inc(small_in, 16)
            sp.dma_start(sgb, sg_bT).then_inc(small_in, 16)
            sp.dma_start(out_g, out_gT).then_inc(small_in, 16)
            sp.dma_start(final_row[:, :], on_all(final_g)).then_inc(final_in, 16)
            for n in range(SLOTS, SLOTS + 3):
                load_group(n)
            sp.wait_ge(h1_ready, NT)
            sp.dma_start(ln_g, on_all(sg_ln_g)).then_inc(ln_in, 16)
            sp.dma_start(ln_b, on_all(sg_ln_b)).then_inc(ln_in, 16)
            for n in range(SLOTS + 3, len(STREAM)):
                load_group(n)
                if STREAM[n] == ("ada", 9):
                    sp.wait_ge(v_var_ready, 1)
                    sp.dma_start(norm2_row, on_all(norm2_g)).then_inc(norm2_in, 16)
                    wait_full(sp, "k", 3)
                    sp.dma_start(sgw, sg_wT).then_inc(sgw_in, 16)
            sp.wait_ge(a2_done, 1)
            sp.dma_start(keysT, sub_keysT).then_inc(keys_in, 16)

            def store_groups(first, last):
                for g in range(first, last):
                    sp.wait_ge(build_read, (g + 1) * GROUP // BATCH)
                    sp.dma_start(g_dram[g], staging[g % 2].rearrange("p i t -> p (i t)")).then_inc(g_stored[g % 2], 16)

            def load_u(I, r):
                sp.dma_start(u_raw[:, r % 2, :], uT[bass.ds(BODY * I + r, 1)].rearrange("b p n -> p (b n)"))\
                    .then_inc(u_in[r % 2], 16)

            def load_v(I, r):
                sp.dma_start(v_raw[:, r % 2, :], expert_v[bass.ds((BODY * I + r) * P, P), :]).then_inc(v_in[r % 2], 16)

            def load_g(I, half):
                src = g_dram[:, :, bass.ds((BODY * I + GLOAD * half) * GROUP, GLOAD * GROUP)]
                sp.dma_start(g_block[:, half].rearrange("p g i t -> p g (i t)"), src.rearrange("g p n -> p g n"))\
                    .then_inc(g_in[half], 16)

            store_groups(0, 2 * GROUPS // DENSE)
            for g in range(4):
                wait_full(sp, "qrow", NT - 1, g)
            for n in range(2):
                load_u(0, n)
            store_groups(2 * GROUPS // DENSE, GROUPS)
            for b in range(2):
                sp.wait_ge(g_stored[b], 16 * GROUPS // 2)
            load_g(0, 0)
            for n in range(2, AHEAD):
                sp.wait_ge(a_full, n - 1)
                load_u(0, n)

            def step(I, r, more, first):
                m = BODY * I + r
                if more:
                    sp.wait_ge(a_full, m + AHEAD - 1)
                    load_u(I + 1, r)
                if not (first and r < 2):
                    sp.wait_ge(v_used, m - 1)
                load_v(I, r)
                if r == 0:
                    if not first:
                        sp.wait_ge(w_made, m)
                    load_g(I, 1)
                if r == GLOAD and more:
                    sp.wait_ge(w_made, m)
                    load_g(I + 1, 0)

            for r in range(BODY):
                step(0, r, True, True)
            with sp.Fori(1, ITERS - 1) as I:
                for r in range(BODY):
                    step(I, r, True, False)
            for r in range(BODY):
                step(ITERS - 1, r, False, False)
            for t in range(NT):
                sp.wait_ge(out_ready, t + 1)
                sp.dma_start(out[t * P:(t + 1) * P, :], xs[:, t, :]).then_inc(stored, 16)
            sp.wait_ge(stored, 16 * NT)

        @block.gpsimd
        def _(pool):
            links = [0]

            def link(ins):
                links[0] += 1
                ins.then_inc(g_chain, 1)
                pool.wait_ge(g_chain, links[0])

            link(nc.gpsimd.memset(ada[:, :], 0.0))
            pool.dma_start(ada[0:1, :], one_row(b_ada)).then_inc(b_ada_in, 16)
            link(nc.gpsimd.memset(ident[:, :], 0.0))
            link(nc.gpsimd.memset(gate[:, :], 1.0))
            link(nc.gpsimd.memset(tri, 1.0))
            nc.gpsimd.iota(iota_u, [[1, TOPK]], base=0, channel_multiplier=0).then_inc(made, 1)
            nc.gpsimd.affine_select(out=ident[:, :], in_=ident[:, :], compare_op=ALU.not_equal, fill=1.0,
                                    base=0, pattern=[[-1, P]], channel_multiplier=1).then_inc(made, 1)
            nc.gpsimd.affine_select(out=tri, in_=tri, compare_op=ALU.is_ge, fill=0.0,
                                    base=0, pattern=[[1, P]], channel_multiplier=-1).then_inc(made, 1)
            wait_full(pool, "h1T", 3, 1)
            nc.gpsimd.memset(q_z, 0.0).then_inc(qz_zero, 1)
            wait_full(pool, "k", 3)
            link(nc.gpsimd.memset(causal, 0.0))
            nc.gpsimd.affine_select(out=causal, in_=causal, compare_op=ALU.is_ge, fill=MASKED,
                                    base=0, pattern=[[-1, P]], channel_multiplier=1).then_inc(causal_made, 1)
            pool.wait_ge(sgw_in, 16)
            nc.gpsimd.affine_select(out=sgw, in_=sgw, compare_op=ALU.is_ge, fill=0.0,
                                    base=0, pattern=[[0, HEADS], [1, P]], channel_multiplier=-1).then_inc(sgw_masked, 1)
            wait_read(pool, "ada", 4)
            wait_read(pool, "ada", 5)
            for g in range(2):
                w = wait_weights(pool, "w_out", g)
                for k in range(KC):
                    nc.gpsimd.tensor_tensor(w[:, k, :], w[:, k, :], gate1[:, g * HALF:(g + 1) * HALF],
                                            ALU.mult).then_inc(w_out_gated, 1)

            wait_read(pool, "O", NT - 1)
            nc.gpsimd.iota(iota128_u, [[1, P]], base=0, channel_multiplier=0).then_inc(iota_made, 1)
            pool.wait_ge(iota_made, 1)
            pool.wait_ge(w_out_gated, 2 * KC)
            nc.gpsimd.tensor_copy(iota128, iota128_u).then_inc(iota_made, 1)
            pool.wait_ge(iota_made, 2)

            def hot_rows(n, i, first):
                for b in range(2):
                    if not first:
                        pool.wait_ge(built, n * BATCHES + 2 * i + b - 1)
                    nc.gpsimd.tensor_copy(j_now[:, b, :], turned[:, n % 2, 1, bass.ds((2 * i + b) * BATCH, BATCH)])\
                        .then_inc(j_staged, 1)
                    pool.wait_ge(j_staged, n * BATCHES + 2 * i + b + 1)
                    pool.sem_inc(hot_granted, 1)
                    for q in range(BATCH):
                        ins = nc.gpsimd.tensor_scalar(hot_j[:, b, q, :], iota128, j_now[:, b, q:q + 1], None, ALU.is_equal)
                    ins.then_inc(hot_j_made, 1)

            for n in range(DENSE):
                wait_read(pool, "turn", n)
                if n == 0:
                    hot_rows(n, 0, True)
                with pool.Fori(1 if n == 0 else 0, BATCHES // 2) as i:
                    hot_rows(n, i, False)

            def gather_rows(table, which, used):
                def one_round(i, half, first):
                    nc.gpsimd.tensor_copy(idx_slot[:, half, :], idx[:, 0, bass.ds((2 * i + half) * STAGED, STAGED)])\
                        .then_inc(idx_staged, 1)
                    pool.wait_ge(idx_staged, which * NSEL // STAGED + 2 * i + half + 1)
                    for r in range(STAGED):
                        if first and r < ROWS:
                            if which:
                                pool.wait_ge(dot_done, NSEL - ROWS + r + 1)
                        else:
                            pool.wait_ge(used, (2 * i + half) * STAGED + r - ROWS + 1 + which)
                        pool.sem_inc(granted, 1)
                        nc.gpsimd.indirect_dma_start(ring[:, r % ROWS, :], None, table,
                                                     bass.IndirectOffsetOnAxis(idx_slot[:, half, r:r + 1], 0))\
                            .then_inc(gathered[r % ROWS], 16)

                one_round(0, 0, True)
                one_round(0, 1, False)
                with pool.Fori(1, NSEL // STAGED // 2) as i:
                    one_round(i, 0, False)
                    one_round(i, 1, False)

            pool.wait_ge(topk_done, 1)
            gather_rows(expert_u, 0, dot_done)
            gather_rows(expert_v, 1, v_added)

        @block.scalar
        def _(act):
            act.wait_ge(c_in, 16)
            nc.scalar.activation(c_exp, c_col, ACT.Exp, scale=-1.0).then_inc(c_exped, 1)
            act.wait_ge(x_in, 16)
            for t in range(NT):
                nc.scalar.activation(y[:, t, :], xs[:, t, :], ACT.Square, accum_out=x_ss[:, t:t + 1]).then_inc(x_squared, 1)
            act.wait_ge(x_mean, 1)
            nc.scalar.activation(x_rms, x_ss, ACT.Sqrt).then_inc(x_root, 1)

            def ada_row(g):
                b = wait_full(act, "ada", g)
                release(nc.scalar.activation(ada[:, g * HALF:(g + 1) * HALF], b[:, :], ACT.Copy), "ada", g)

            def copy_chunks(dst, name, func=ACT.Copy):
                b = wait_full(act, *name)
                release(nc.scalar.activation(dst, b[:, :].rearrange("p (k t) -> p k t", k=4), func), *name)

            for g in range(4):
                ada_row(g)
            act.wait_ge(a1_done, 1)
            for t in range(NT):
                for s in range(2):
                    copy_chunks(hT[:, 4 * s:4 * s + 4, t * P:(t + 1) * P], ("h1T", t, s))
            for t in range(NT):
                b = wait_full(act, "zv", t)
                release(nc.scalar.activation(y[:, t, HALF:D], b[:, :], ACT.Gelu), "zv", t)
            act.wait_ge(f_abs, 1)
            nc.scalar.activation(lsg_e, lsg_e, ACT.Exp, scale=-1.0).then_inc(f_exp, 1)
            act.wait_ge(f_plus, 1)
            nc.scalar.activation(lsg_e, lsg_e, ACT.Ln).then_inc(f_log, 1)
            for t in range(NT):
                b = wait_full(act, "zu", t)
                release(nc.scalar.activation(y[:, t, 0:HALF], b[:, :], ACT.Gelu), "zu", t)
            act.wait_ge(qz_zero, 1)
            for n in range(4):
                b = wait_full(act, "q", n)
                nc.scalar.activation(q_z[0:DH, 2 * n, :], b[0:DH, :], ACT.Copy, scale=DH ** -0.5)
                release(nc.scalar.activation(q_z[DH:P, 2 * n + 1, :], b[DH:P, :], ACT.Copy, scale=DH ** -0.5), "q", n)
            act.wait_ge(v_var_ready, 1)
            nc.scalar.activation(v_var, v_var, ACT.Sqrt).then_inc(v_root, 1)
            for g in range(4, 12):
                ada_row(g)
            b = wait_full(act, "cum")
            release(nc.scalar.activation(ncum, b[0:HEADS, :], ACT.Copy, scale=-1.0), "cum")

            for n, (qt, h) in enumerate(ATTN):
                keys = (qt + 1) * P
                act.wait_ge(neg_max, n + 1)
                if n >= 2:
                    wait_full(act, "PT", n - 2)
                release(nc.scalar.activation(p_exp[:, n % 2, 0:keys], bank[place["S", n][0]][:, 0:keys], ACT.Exp,
                                             bias=nmax[:, n:n + 1], accum_out=rsum[:, n:n + 1]),
                        "S", n)

            wait_read(act, "O", NT - 1)
            for t in range(NT):
                nc.scalar.activation(squares[:, t, :], y[:, t, :], ACT.Square).then_inc(y_squared, 1)
            for t in range(NT):
                act.wait_ge(y_mean, t + 1)
                nc.scalar.activation(y_rms[:, t], y_var[:, t], ACT.Sqrt).then_inc(y_root, 1)

            def x1_roots(t):
                act.wait_ge(x1_mean, t + 1)
                nc.scalar.activation(x1_rms[:, t:t + 1], x1_ss[:, t:t + 1], ACT.Sqrt).then_inc(x1_root, 1)

            for t in range(NT):
                wait_read(act, "mix", t, 0)
                wait_read(act, "mix", t, 1)
                nc.scalar.activation(squares[:, t, :], xs[:, t, :], ACT.Square, accum_out=x1_ss[:, t:t + 1]).then_inc(x1_squared, 1)
                if t:
                    x1_roots(t - 1)
            x1_roots(NT - 1)
            for t in range(NT):
                wait_full(act, "h2T", t, 1)
                for s in range(2):
                    copy_chunks(h2T(t)[:, 4 * s:4 * s + 4, :], ("h2T", t, s))

            def query(n):
                if n >= 2:
                    wait_full(act, "turn", n - 2)
                for g in range(4):
                    b = wait_full(act, "qrow", n, g)
                    release(nc.scalar.activation(qrow(n)[:, g * HALF:(g + 1) * HALF], b[:, :], ACT.Copy), "qrow", n, g)
                for g in range(4):
                    copy_chunks(qT(n)[:, 4 * g:4 * g + 4, :], ("qT", n, g))
                for g in range(4):
                    copy_chunks(scores(n)[:, 4 * g:4 * g + 4, :], ("score", n, g))

            def gate_exps(n):
                act.wait_ge(best_ready, n + 1)
                nc.scalar.activation(gate[:, :], gate[:, :], ACT.Exp).then_inc(gate_exp, 1)

            def build(n):
                if n >= 2:
                    act.wait_ge(build_read, (n - 1) * BATCHES)
                b = wait_full(act, "turn", n)
                release(nc.scalar.activation(turned[:, n % 2], b[:, 0:3 * P].rearrange("p (c t) -> p c t", c=3), ACT.Copy), "turn", n)
                per_group = GROUP // BATCH
                for g in range(P // GROUP):
                    group = n * P // GROUP + g
                    if group >= 2:
                        act.wait_ge(g_stored[group % 2], 16 * (group // 2))
                    with act.Fori(0, per_group // 2) as i:
                        for b in range(2):
                            act.wait_ge(built, group * per_group + 2 * i + b + 1)
                            act.sem_inc(build_granted, 1)
                            out_t = staging[group % 2][:, :, bass.ds((2 * i + b) * BATCH, BATCH)]
                            nc.scalar.activation(out_t, bank[6 + b][:, :].rearrange("p (t i) -> p i t", t=BATCH), ACT.Copy)\
                                .then_inc(build_read, 1)

            query(0)
            for n in range(DENSE):
                query(n + 1)
                gate_exps(n)
                build(n)

            for d in range(DENSE):
                wait_read(act, "h2T", ORDER[d], 0)
                wait_read(act, "h2T", ORDER[d], 1)
                nc.scalar.activation(h2_hi[:, d], h2T(ORDER[d]), ACT.Copy).then_inc(h2_hi_made, 1)

            def round_u(I, r):
                act.wait_ge(u_in[r % 2], 16 * (BODY // 2 * I + r // 2 + 1))
                nc.scalar.activation(u_hi[:, r % 2, :], u_raw[:, r % 2, :], ACT.Copy).then_inc(u_hi_made, 1)

            def gelu(I, r):
                act.wait_ge(a_full, BODY * I + r + 1)
                nc.scalar.activation(ahead[:, r, :], bank[r % 2][:, 0:DTOK], ACT.Gelu).then_inc(a_read, 1)

            for n in range(AHEAD):
                round_u(0, n)
                if n:
                    gelu(0, n - 1)
            gate_exps(NT - 1)

            def step(I, r, more):
                m = BODY * I + r
                if more:
                    round_u(I + 1, r)
                act.wait_ge(v_in[r % 2], 16 * (BODY // 2 * I + r // 2 + 1))
                nc.scalar.activation(v_hi[:, r % 2, :], v_raw[:, r % 2, :], ACT.Copy).then_inc(v_hi_made, 1)
                act.wait_ge(w_made, m + 1)
                nc.scalar.activation(w_hi[:, r % 2, :], w_raw[:, r % 2, :], ACT.Copy).then_inc(w_hi_made, 1)
                if r == 0:
                    gelu(I, AHEAD - 1)
                elif more:
                    gelu(I + 1, r - 1)

            with act.Fori(0, ITERS // 2) as I:
                for r in range(BODY):
                    step(I, r, True)
            act.wait_ge(dot_done, NSEL)
            nc.scalar.activation(act_w[:, :], act_w[:, :], ACT.Gelu).then_inc(gelu_done, 1)
            with act.Fori(ITERS // 2, ITERS - 1) as I:
                for r in range(BODY):
                    step(I, r, True)
            for r in range(BODY):
                step(ITERS - 1, r, False)

            for t in range(NT):
                act.wait_ge(x2_ready, t + 1)
                nc.scalar.activation(y[:, t, :], xs[:, t, :], ACT.Square, accum_out=x2_ss[:, t:t + 1]).then_inc(x2_squared, 1)
                act.wait_ge(x2_mean, t + 1)
                nc.scalar.activation(x2_rms[:, t:t + 1], x2_ss[:, t:t + 1], ACT.Sqrt).then_inc(x2_root, 1)

        @block.tensor
        def _(pe):
            def start(*name):
                b, n = place[name]
                if n > 1:
                    pe.wait_ge(read[b], n - 1)
                return bank[b]

            def done(ins, *name):
                ins.then_inc(full[place[name][0]], 1)

            def ada_row(g):
                pe.wait_ge(ada_summed, g + 1)
                b = start("ada", g)
                done(nc.tensor.matmul(b[:, :], ones, ada[:, g * HALF:(g + 1) * HALF], start=True, stop=True), "ada", g)

            def transposes(name, blocks):
                b = start(*name)
                for j, blk in enumerate(blocks):
                    ins = nc.tensor.transpose(b[:, j * P:(j + 1) * P], blk, ident[:, :])
                done(ins, *name)

            pe.wait_ge(made, 3)
            for g in range(4):
                ada_row(g)
            for t in range(NT):
                pe.wait_ge(h1_ready, t + 1)
                for s in range(2):
                    transposes(("h1T", t, s), [h1[:, t, (4 * s + j) * P:(4 * s + j + 1) * P] for j in range(4)])

            for g in ("zv", "v", "f", "zu"):
                if g == "f":
                    pe.wait_ge(fw_in, 16)
                    b = start("f")
                    for t in range(NT):
                        for k in range(KC):
                            ins = nc.tensor.matmul(b[:, t * HEADS:(t + 1) * HEADS], hT[:, k, t * P:(t + 1) * P],
                                                   f_w[:, k, :], start=(k == 0), stop=(k == KC - 1))
                    done(ins, "f")
                    continue
                w = wait_weights(pe, "w_in", g)
                for t in range(NT):
                    wait_read(pe, "h1T", t, 1)
                    wait_read(pe, "h1T", t, 0)
                    b = start(g, t)
                    for k in range(KC):
                        ins = nc.tensor.matmul(b[:, :], hT[:, k, t * P:(t + 1) * P], w[:, k, :],
                                               start=(k == 0), stop=(k == KC - 1))
                    done(ins, g, t)
            for g in ("q", "k"):
                w = wait_weights(pe, "w_in", g)
                for n in range(4):
                    b = start(g, n)
                    for k in range(KC):
                        ins = nc.tensor.matmul(b[:, :], w[:, k, n * P:(n + 1) * P], hT[:, k, :],
                                               start=(k == 0), stop=(k == KC - 1))
                    done(ins, g, n)
            for g in range(4, 12):
                ada_row(g)

            pe.wait_ge(f_done, 1)
            b = start("cum")
            for kt in range(NT):
                for st in range(kt + 1):
                    ins = nc.tensor.matmul(b[0:HEADS, kt * P:(kt + 1) * P], lsg[:, st * HEADS:(st + 1) * HEADS],
                                           tri if st == kt else ones, start=(st == 0), stop=(st == kt))
            done(ins, "cum")

            pe.wait_ge(sgw_masked, 1)
            pe.wait_ge(v_norm, 1)
            for n in range(4):
                b = start("sgu", n)
                for j in range(2):
                    h = 2 * n + j
                    ins = nc.tensor.matmul(b[:, j * 256:(j + 1) * 256].rearrange("p (t d) -> p t d", t=NT), sgw[:, h, :],
                                           y[:, :, HALF + h * DH:HALF + (h + 1) * DH], start=True, stop=True)
                done(ins, "sgu", n)

            def logits(n):
                qt, h = ATTN[n]
                keys = (qt + 1) * P
                b = start("S", n)
                nc.tensor.matmul(b[:, 0:keys], q_z[:, h, qt * P:(qt + 1) * P], kT[:, h // 2, 0:keys],
                                 start=True, stop=False)
                done(nc.tensor.matmul(b[:, 0:keys], ident[0:HEADS, h:h + 1].broadcast_to([HEADS, P]), ncum[:, 0:keys],
                                      start=False, stop=True), "S", n)

            def turn(n):
                qt, h = ATTN[n]
                wait_read(pe, "S", n)
                transposes(("PT", n), [p_exp[:, n % 2, kb * P:(kb + 1) * P] for kb in range(qt + 1)])

            def values(n):
                qt, h = ATTN[n]
                wait_read(pe, "PT", n)
                b = start("O", qt) if h == 0 else bank[place["O", qt][0]]
                for kb in range(qt + 1):
                    ins = nc.tensor.matmul(b[:, h * DH:(h + 1) * DH], p_T[:, n % 2, kb * P:(kb + 1) * P],
                                           v_tok[:, kb, h * DH:(h + 1) * DH], start=(kb == 0), stop=(kb == qt))
                if h == HEADS - 1:
                    done(ins, "O", qt)
                else:
                    ins.then_inc(pT_used, 1)

            wait_read(pe, "cum")
            wait_read(pe, "q", 3)
            wait_read(pe, "k", 3)
            wait_read(pe, "v", 3)
            for n in range(len(ATTN) + 2):
                if n < len(ATTN):
                    logits(n)
                if 1 <= n <= len(ATTN):
                    turn(n - 1)
                if n >= 2:
                    values(n - 2)

            for t in range(NT):
                pe.wait_ge(y_ready, t + 1)
                for s in range(2):
                    transposes(("yT", t, s), [y[:, t, (4 * s + j) * P:(4 * s + j + 1) * P] for j in range(4)])
            pe.wait_ge(w_out_gated, 2 * KC)
            for t in range(NT):
                wait_read(pe, "yT", t, 0)
                wait_read(pe, "yT", t, 1)
                for s in range(2):
                    w = weights[:, slot_of["w_out", s], :, :]
                    b = start("mix", t, s)
                    for k in range(KC):
                        ins = nc.tensor.matmul(b[:, :], yT[:, t, k, :], w[:, k, :], start=(k == 0), stop=(k == KC - 1))
                    done(ins, "mix", t, s)
            for t in range(NT):
                pe.wait_ge(h2_ready, t + 1)
                for s in range(2):
                    transposes(("h2T", t, s), [y[:, t, (4 * s + j) * P:(4 * s + j + 1) * P] for j in range(4)])

            def query(n):
                t = ORDER[n]
                wait_read(pe, "h2T", t, 0)
                wait_read(pe, "h2T", t, 1)
                for g in range(4):
                    w = wait_weights(pe, "w_query", g)
                    b = start("qrow", n, g)
                    for k in range(KC):
                        ins = nc.tensor.matmul(b[:, :], h2T(t)[:, k, :], w[:, k, :], start=(k == 0), stop=(k == KC - 1))
                    done(ins, "qrow", n, g)
                for g in range(4):
                    wait_read(pe, "qrow", n, g)
                    transposes(("qT", n, g), [qrow(n)[:, (4 * g + j) * P:(4 * g + j + 1) * P] for j in range(4)])
                pe.wait_ge(keys_in, 16)
                for g in range(4):
                    wait_read(pe, "qT", n, g)
                    b = start("score", n, g)
                    for j in range(4):
                        p = 4 * g + j
                        ins = nc.tensor.matmul(b[:, j * P:(j + 1) * P], qT(n)[:, p, :], keysT[:, p, :], start=True, stop=True)
                    done(ins, "score", n, g)

            def build(n):
                if n:
                    pe.wait_ge(build_read, n * BATCHES)
                pe.wait_ge(gates_ready, n + 1)
                transposes(("turn", n), [picks(n)[2], picks(n)[3], gate[:, :]])
                wait_read(pe, "turn", n)

                def batches(i, first):
                    for b in range(2):
                        m = n * BATCHES + 2 * i + b
                        pe.wait_ge(hot_j_made, m + 1)
                        pe.wait_ge(hot_i_made, m + 1)
                        if not first:
                            pe.wait_ge(build_read, m - 1)
                        for q in range(BATCH):
                            ins = nc.tensor.matmul(bank[6 + b][:, q * P:(q + 1) * P], hot_j[:, b, q, :], hot_i[:, b, q, :],
                                                   start=True, stop=True)
                        ins.then_inc(built, 1)

                if n == 0:
                    wait_read(pe, "h2T", NT - 1, 1)
                    batches(0, True)
                with pe.Fori(1 if n == 0 else 0, BATCHES // 2) as i:
                    batches(i, False)

            query(0)
            for n in range(DENSE):
                query(n + 1)
                build(n)

            def products(I, r, first=False):
                m = BODY * I + r
                pe.wait_ge(u_lo_made, m + 1)
                if not (first and r < 2):
                    pe.wait_ge(a_read, m - 1)
                a = bank[r % 2][:, 0:DTOK].rearrange("p (d t) -> p d t", d=DENSE)
                uh = u_hi[:, r % 2, :].rearrange("p (k e) -> p k e", k=KC)
                ul = u_lo[:, r % 2, :].rearrange("p (k e) -> p k e", k=KC)
                for k in range(KC):
                    nc.tensor.matmul(a, uh[:, k, :], h2_hi[:, :, k, :], start=(k == 0), stop=False)
                    nc.tensor.matmul(a, uh[:, k, :], h2_lo[:, :, k, :], start=False, stop=False)
                    ins = nc.tensor.matmul(a, ul[:, k, :], h2_hi[:, :, k, :], start=False, stop=(k == KC - 1))
                ins.then_inc(a_full, 1)

            def outputs(I, r, begin, end):
                m = BODY * I + r
                pe.wait_ge(v_lo_made, m + 1)
                pe.wait_ge(w_lo_made, m + 1)
                for d in range(DENSE):
                    wh = w_hi[:, r % 2, d * P:(d + 1) * P]
                    wl = w_lo[:, r % 2, d * P:(d + 1) * P]
                    for s in range(2):
                        acc, cols = bank[2 + 2 * d + s][:, :], slice(s * HALF, (s + 1) * HALF)
                        nc.tensor.matmul(acc, wh, v_hi[:, r % 2, cols], start=begin, stop=False)
                        nc.tensor.matmul(acc, wh, v_lo[:, r % 2, cols], start=False, stop=False)
                    for s in range(2):
                        acc, cols = bank[2 + 2 * d + s][:, :], slice(s * HALF, (s + 1) * HALF)
                        ins = nc.tensor.matmul(acc, wl, v_hi[:, r % 2, cols], start=False, stop=end)
                ins.then_inc(v_used, 1)

            pe.wait_ge(h2_lo_made, DENSE)
            for g in range(4):
                wait_read(pe, "score", NT - 1, g)
            for g in (2, 3):
                wait_read(pe, "qT", NT - 1, g)
            for n in range(AHEAD):
                products(0, n, True)
            pe.wait_ge(build_read, DENSE * BATCHES)
            for r in range(BODY):
                products(1, r)
                outputs(0, r, r == 0, False)
            with pe.Fori(1, ITERS - 1) as I:
                for r in range(BODY):
                    products(I + 1, r)
                    outputs(I, r, False, False)
            for r in range(BODY):
                outputs(ITERS - 1, r, False, r == BODY - 1)

        @block.vector
        def _(dve):
            links = [0]

            def link(ins):
                links[0] += 1
                ins.then_inc(v_chain, 1)
                dve.wait_ge(v_chain, links[0])

            tt, ts, stt = nc.vector.tensor_tensor, nc.vector.tensor_scalar, nc.vector.scalar_tensor_tensor

            dve.wait_ge(c_exped, 1)
            link(ts(c_exp, c_exp, 1.0, None, ALU.add))
            link(nc.vector.reciprocal(c_exp, c_exp))
            link(tt(c_act, c_col, c_exp, ALU.mult))

            def ada_sum(g):
                w = wait_weights(dve, "ada", g)
                acc = ada[:, g * HALF:(g + 1) * HALF]
                for k in range(KC):
                    ins = stt(out=acc, in0=w[:, k, :], scalar=c_act[:, k:k + 1], in1=acc, op0=ALU.mult, op1=ALU.add)
                    if k < KC - 1:
                        link(ins)
                ins.then_inc(ada_summed, 1)

            dve.wait_ge(b_ada_in, 16)
            for g in range(4):
                ada_sum(g)
            dve.wait_ge(x_squared, NT)
            ts(x_ss, x_ss, 1.0 / D, EPS, ALU.mult, ALU.add).then_inc(x_mean, 1)
            dve.wait_ge(x_root, 1)
            link(nc.vector.reciprocal(x_rms, x_rms))
            dve.wait_ge(made, 3)
            link(nc.vector.tensor_copy(iota16, iota_u))
            for g in range(4):
                wait_read(dve, "ada", g)
            dve.wait_ge(norm1_in, 16)
            stt(out=scale1, in0=scale1, scalar=1.0, in1=norm1_row, op0=ALU.add, op1=ALU.mult).then_inc(a1_done, 1)
            dve.wait_ge(a1_done, 1)
            for t in range(NT):
                link(stt(out=h1[:, t, :], in0=xs[:, t, :], scalar=x_rms[:, t:t + 1], in1=scale1, op0=ALU.mult, op1=ALU.mult))
                tt(h1[:, t, :], h1[:, t, :], shift1, ALU.add).then_inc(h1_ready, 1)
            for t in range(NT):
                b = wait_full(dve, "v", t)
                release(nc.vector.tensor_copy(v_tok[:, t, :], b[:, :]), "v", t)

            b = wait_full(dve, "f")
            dve.wait_ge(small_in, 48)
            ins = tt(logit.rearrange("p (t h) -> p t h", t=NT), b[:, 0:32].rearrange("p (t h) -> p t h", t=NT),
                     bf_row.unsqueeze(1).broadcast_to([P, NT, HEADS]), ALU.add)
            release(ins, "f")
            wait_read(dve, "f")
            stt(out=lsg_e, in0=logit, scalar=-1.0, in1=logit, op0=ALU.mult, op1=ALU.max).then_inc(f_abs, 1)
            dve.wait_ge(f_exp, 1)
            ts(lsg_e, lsg_e, 1.0, None, ALU.add).then_inc(f_plus, 1)
            dve.wait_ge(f_log, 1)
            stt(out=lsg, in0=logit, scalar=0.0, in1=lsg_e, op0=ALU.min, op1=ALU.subtract).then_inc(f_done, 1)

            zv = y[:, :, HALF:D].rearrange("p t (h d) -> p t h d", h=HEADS)

            def per_head(s):
                return s.rearrange("p (t h) -> p t h", t=NT)

            def over_head(s):
                return per_head(s).unsqueeze(3).broadcast_to([P, NT, HEADS, DH])

            wait_read(dve, "zv", NT - 1)
            link(nc.vector.tensor_reduce(per_head(v_mean), zv, AX_X, ALU.add))
            link(ts(v_mean, v_mean, -1.0 / DH, None, ALU.mult))
            for t in range(NT):
                ins = tt(zv[:, t], zv[:, t], per_head(v_mean)[:, t].unsqueeze(2).broadcast_to([P, HEADS, DH]), ALU.add)
            link(ins)
            sq = v_sq.rearrange("p (t d) -> p t d", t=2)
            for n in range(2):
                link(tt(sq, y[:, 2 * n:2 * n + 2, HALF:D], y[:, 2 * n:2 * n + 2, HALF:D], ALU.mult))
                link(nc.vector.tensor_reduce(v_var[:, 16 * n:16 * n + 16], v_sq.rearrange("p (g d) -> p g d", d=DH), AX_X, ALU.add))
            ts(v_var, v_var, 1.0 / DH, EPS, ALU.mult, ALU.add).then_inc(v_var_ready, 1)
            for g in range(4, 7):
                ada_sum(g)
            for n in range(4):
                b = wait_full(dve, "k", n)
                release(nc.vector.tensor_copy(kT[:, n, :], b[:, :]), "k", n)
            dve.wait_ge(v_root, 1)
            link(nc.vector.reciprocal(v_var, v_var))
            for t in range(NT):
                ins = tt(zv[:, t], zv[:, t], per_head(v_var)[:, t].unsqueeze(2).broadcast_to([P, HEADS, DH]), ALU.mult)
            link(ins)
            dve.wait_ge(ln_in, 32)
            zvf = y[:, :, HALF:D]
            link(tt(zvf, zvf, ln_g.unsqueeze(1).broadcast_to([P, NT, HALF]), ALU.mult))
            tt(zvf, zvf, ln_b.unsqueeze(1).broadcast_to([P, NT, HALF]), ALU.add).then_inc(v_norm, 1)
            for g in range(7, 12):
                ada_sum(g)
            for g in range(8, 10):
                wait_read(dve, "ada", g)
            dve.wait_ge(norm2_in, 16)
            stt(out=scale2, in0=scale2, scalar=1.0, in1=norm2_row, op0=ALU.add, op1=ALU.mult).then_inc(a2_done, 1)

            wait_read(dve, "zu", NT - 1)
            for n in range(4):
                b = wait_full(dve, "sgu", n)
                for j in range(2):
                    h = 2 * n + j
                    zu = y[:, :, h * DH:(h + 1) * DH]
                    ins = stt(out=zu, in0=b[:, j * 256:(j + 1) * 256].rearrange("p (t d) -> p t d", t=NT),
                              scalar=sgb[:, h:h + 1], in1=zu, op0=ALU.add, op1=ALU.mult)
                release(ins, "sgu", n)

            def row_max(n):
                qt, h = ATTN[n]
                keys = (qt + 1) * P
                b = wait_full(dve, "S", n)
                own = b[:, qt * P:keys]
                link(tt(own, own, causal, ALU.add))
                nc.vector.tensor_reduce(nmax[:, n:n + 1], b[:, 0:keys], AX_X, ALU.max, negate=True).then_inc(neg_max, 1)

            def copy_turned(n):
                qt, h = ATTN[n]
                b = wait_full(dve, "PT", n)
                if n >= 2:
                    was_qt, was_h = ATTN[n - 2]
                    if was_h == HEADS - 1:
                        wait_full(dve, "O", was_qt)
                    else:
                        dve.wait_ge(pT_used, was_qt * (HEADS - 1) + was_h + 1)
                release(nc.vector.tensor_copy(p_T[:, n % 2, 0:(qt + 1) * P], b[:, 0:(qt + 1) * P]), "PT", n)

            def output(qt):
                b = wait_full(dve, "O", qt)
                rs = slice(qt * HEADS, (qt + 1) * HEADS)
                for n in (-2, -1):
                    wait_read(dve, "S", (qt + 1) * HEADS + n)
                link(nc.vector.reciprocal(o_scale[:, rs], rsum[:, rs]))
                release(tt(y[:, qt, HALF:D].rearrange("p (h d) -> p h d", h=HEADS),
                           b[:, :].rearrange("p (h d) -> p h d", h=HEADS),
                           o_scale[:, rs].unsqueeze(2).broadcast_to([P, HEADS, DH]), ALU.mult), "O", qt)

            dve.wait_ge(causal_made, 1)
            for n in range(len(ATTN) + 2):
                if n < len(ATTN):
                    row_max(n)
                if 1 <= n <= len(ATTN):
                    copy_turned(n - 1)
                if n >= 2 and ATTN[n - 2][1] == HEADS - 1:
                    output(ATTN[n - 2][0])

            def head_norm(t):
                dve.wait_ge(y_root, t + 1)
                link(nc.vector.reciprocal(y_rms[:, t], y_rms[:, t]))
                yh = y[:, t, :].rearrange("p (h d) -> p h d", d=DH)
                tt(yh, yh, y_rms[:, t].unsqueeze(2).broadcast_to([P, 2 * HEADS, DH]), ALU.mult).then_inc(y_ready, 1)

            def residual(t):
                for s in range(2):
                    b = wait_full(dve, "mix", t, s)
                    xh = xs[:, t, s * HALF:(s + 1) * HALF]
                    release(tt(xh, b[:, :], xh, ALU.add), "mix", t, s)

            def x1_stat(t):
                dve.wait_ge(x1_squared, t + 1)
                ts(x1_ss[:, t:t + 1], x1_ss[:, t:t + 1], 1.0 / D, EPS, ALU.mult, ALU.add).then_inc(x1_mean, 1)

            def second_norm(t):
                dve.wait_ge(x1_root, t + 1)
                link(nc.vector.reciprocal(x1_rms[:, t:t + 1], x1_rms[:, t:t + 1]))
                link(stt(out=y[:, t, :], in0=xs[:, t, :], scalar=x1_rms[:, t:t + 1], in1=scale2, op0=ALU.mult, op1=ALU.mult))
                tt(y[:, t, :], y[:, t, :], shift2, ALU.add).then_inc(h2_ready, 1)

            for t in range(NT):
                dve.wait_ge(y_squared, t + 1)
                link(nc.vector.tensor_reduce(y_var[:, t], squares[:, t, :].rearrange("p (h d) -> p h d", d=DH), AX_X, ALU.add))
                ts(y_var[:, t], y_var[:, t], 1.0 / DH, EPS, ALU.mult, ALU.add).then_inc(y_mean, 1)
            for t in range(NT):
                head_norm(t)
            for t in range(NT):
                for s in range(2):
                    b = wait_full(dve, "yT", t, s)
                    release(tt(yT[:, t, 4 * s:4 * s + 4, :], b[:, :].rearrange("p (k t) -> p k t", k=4),
                               out_g[:, 4 * s:4 * s + 4].unsqueeze(2).broadcast_to([P, 4, P]), ALU.mult), "yT", t, s)
            for t in range(NT + 2):
                if t < NT:
                    residual(t)
                if 1 <= t <= NT:
                    x1_stat(t - 1)
                if t >= 2:
                    second_norm(t - 2)

            def top16(values_out, index_out, rows, groups):
                for g in range(groups):
                    ins = nc.vector.max(values_out[:, g, 0:8], rows[:, g, :])
                link(ins)
                for g in range(groups):
                    ins = nc.vector.max_index(index_out[:, g, 0:8], values_out[:, g, 0:8], rows[:, g, :])
                link(ins)
                yield
                for g in range(groups):
                    ins = nc.vector.match_replace(rows[:, g, :], values_out[:, g, 0:8], rows[:, g, :], TAKEN)
                link(ins)
                yield
                for g in range(groups):
                    ins = nc.vector.max(values_out[:, g, 8:16], rows[:, g, :])
                link(ins)
                for g in range(groups):
                    ins = nc.vector.max_index(index_out[:, g, 8:16], values_out[:, g, 8:16], rows[:, g, :])
                link(ins)

            def retrieve(n):
                cand = cand_of(n)
                pos_a, pos_b, sel_i, sel_j, pos_u = picks(n)
                for g in range(4):
                    wait_read(dve, "score", n, g)
                yield from top16(top_v, top_i, scores(n), HP)
                yield
                halves_v = top_v.rearrange("p (h s) k -> p h s k", s=2)
                link(tt(cand.rearrange("p h (a b) -> p h a b", b=TOPK),
                        halves_v[:, :, 0, :].unsqueeze(3).broadcast_to([P, PH, TOPK, TOPK]),
                        halves_v[:, :, 1, :].unsqueeze(2).broadcast_to([P, PH, TOPK, TOPK]), ALU.add))
                yield from top16(best_v, best_p, cand, PH)
                yield
                if n:
                    wait_full(dve, "turn", n - 1)
                tt(gate[:, :].rearrange("p (h k) -> p h k", h=PH), best_v,
                   best_v[:, :, 0:1].broadcast_to([P, PH, TOPK]), ALU.subtract).then_inc(best_ready, 1)
                link(nc.vector.tensor_copy(top_f, top_i))
                flat_p = best_p.rearrange("p h k -> p (h k)")
                half_f = top_f.rearrange("p (h s) k -> p h s k", s=2)
                for s, place_f, picked in ((0, pos_a, sel_i), (1, pos_b, sel_j)):
                    if s == 0:
                        link(ts(pos_u.bitcast(U32), flat_p, 4, None, ALU.logical_shift_right))
                    else:
                        link(ts(pos_u.bitcast(U32), flat_p, 15, None, ALU.bitwise_and))
                    link(nc.vector.tensor_copy(place_f, pos_u.bitcast(U32)))
                    for hh in range(2):
                        sel = slice(64 * hh, 64 * hh + 64)
                        link(tt(onehot, place_f[:, sel].unsqueeze(2).broadcast_to([P, 64, TOPK]),
                                iota16.unsqueeze(1).broadcast_to([P, 64, TOPK]), ALU.is_equal))
                        oh = onehot.rearrange("p (h k) a -> p h k a", h=4)
                        link(tt(oh, oh, half_f[:, 4 * hh:4 * hh + 4, s, :].unsqueeze(2).broadcast_to([P, 4, TOPK, TOPK]),
                                ALU.mult))
                        link(nc.vector.tensor_reduce(picked[:, sel], onehot, AX_X, ALU.add))
                    if s == 0:
                        yield
                if ORDER[n] == SPARSE:
                    stt(out=idx[:, 0, :], in0=sel_i, scalar=float(NKEYS), in1=sel_j, op0=ALU.mult, op1=ALU.add)\
                        .then_inc(topk_done, 1)

            def gates(n):
                dve.wait_ge(gate_exp, n + 1)
                gh = gate[:, :].rearrange("p (h k) -> p h k", h=PH)
                link(nc.vector.tensor_reduce(gate_sum, gh, AX_X, ALU.add))
                link(nc.vector.reciprocal(gate_sum, gate_sum))
                tt(gh, gh, gate_sum.unsqueeze(2).broadcast_to([P, PH, TOPK]), ALU.mult).then_inc(gates_ready, 1)

            def hot_rows(n, i, first):
                for b in range(2):
                    if not first:
                        dve.wait_ge(built, n * BATCHES + 2 * i + b - 1)
                    for q in range(BATCH):
                        at = (2 * i + b) * BATCH + q
                        ins = ts(hot_i[:, b, q, :], iota128, turned[:, n % 2, 0, bass.ds(at, 1)],
                                 turned[:, n % 2, 2, bass.ds(at, 1)], ALU.is_equal, ALU.mult)
                    ins.then_inc(hot_i_made, 1)

            dve.wait_ge(h2_ready, NT)
            for n in range(DENSE):
                for _step in retrieve(n):
                    pass
                gates(n)
                wait_read(dve, "turn", n)
                if n == 0:
                    dve.wait_ge(iota_made, 2)
                    hot_rows(n, 0, True)
                with dve.Fori(1 if n == 0 else 0, BATCHES // 2) as i:
                    hot_rows(n, i, False)

            wait_full(dve, "qrow", NT - 1, 0)
            for d in range(DENSE):
                dve.wait_ge(h2_hi_made, d + 1)
                tt(h2_lo[:, d], h2T(ORDER[d]), h2_hi[:, d].bitcast(F32), ALU.subtract).then_inc(h2_lo_made, 1)

            def rest_of_u(I, r):
                dve.wait_ge(u_hi_made, BODY * I + r + 1)
                tt(u_lo[:, r % 2, :], u_raw[:, r % 2, :], u_hi[:, r % 2, :].bitcast(F32), ALU.subtract).then_inc(u_lo_made, 1)

            steps = retrieve(NT - 1)
            for n in range(AHEAD):
                rest_of_u(0, n)
                next(steps, None)
            for _step in steps:
                pass
            gates(NT - 1)

            def sparse_rows(I, r, adding):
                for q in range(STEP_ROWS):
                    at = STEP_ROWS * r + q
                    per_body = STEP_ROWS * BODY
                    dve.wait_ge(gathered[at % ROWS], 16 * (per_body // ROWS * I + at // ROWS + 1))
                    gathered_row = ring[:, at % ROWS, :]
                    if not adding:
                        stt(out=gathered_row, in0=gathered_row, scalar=1.0, in1=y[:, SPARSE, :], op0=ALU.mult, op1=ALU.mult,
                            accum_out=act_w[:, bass.ds(per_body * I + at, 1)]).then_inc(dot_done, 1)
                        continue
                    n = per_body * (I - ITERS // 2) + at
                    dve.wait_ge(v_added, n + 1)
                    stt(out=y[:, SPARSE, :], in0=gathered_row, scalar=act_w[:, bass.ds(n, 1)], in1=y[:, SPARSE, :],
                        op0=ALU.mult, op1=ALU.add).then_inc(v_added, 1)

            def step(I, r, more, first, adding):
                m = BODY * I + r
                if more:
                    rest_of_u(I + 1, r)
                dve.wait_ge(a_read, m + 1)
                if r % GLOAD == 0:
                    dve.wait_ge(g_in[r // GLOAD], 16 * (I + 1))
                if not (first and r < 2):
                    dve.wait_ge(v_used, m - 1)
                grouped = "p (g t) -> p g t"
                tt(w_raw[:, r % 2, :].rearrange(grouped, g=GROUPS), ahead[:, r, :].rearrange(grouped, g=GROUPS),
                   g_block[:, r // GLOAD, :, r % GLOAD, :], ALU.mult).then_inc(w_made, 1)
                dve.wait_ge(v_hi_made, m + 1)
                tt(v_lo[:, r % 2, :], v_raw[:, r % 2, :], v_hi[:, r % 2, :].bitcast(F32), ALU.subtract).then_inc(v_lo_made, 1)
                dve.wait_ge(w_hi_made, m + 1)
                tt(w_lo[:, r % 2, :], w_raw[:, r % 2, :], w_hi[:, r % 2, :].bitcast(F32), ALU.subtract).then_inc(w_lo_made, 1)
                sparse_rows(I, r, adding)

            for r in range(BODY):
                step(0, r, True, True, False)
            with dve.Fori(1, ITERS // 2) as I:
                for r in range(BODY):
                    step(I, r, True, False, False)
            dve.wait_ge(gelu_done, 1)
            tt(act_w[:, :], act_w[:, :], gate[:, :], ALU.mult).then_inc(w_ready, 1)
            dve.wait_ge(dot_done, NSEL)
            dve.wait_ge(w_ready, 1)
            nc.vector.memset(y[:, SPARSE, :], 0.0).then_inc(v_added, 1)
            with dve.Fori(ITERS // 2, ITERS - 1) as I:
                for r in range(BODY):
                    step(I, r, True, False, True)
            for r in range(BODY):
                step(ITERS - 1, r, False, False, True)

            def finish(t):
                dve.wait_ge(x2_squared, t + 1)
                ts(x2_ss[:, t:t + 1], x2_ss[:, t:t + 1], 1.0 / D, EPS, ALU.mult, ALU.add).then_inc(x2_mean, 1)
                dve.wait_ge(x2_root, t + 1)
                link(nc.vector.reciprocal(x2_rms[:, t:t + 1], x2_rms[:, t:t + 1]))
                stt(out=xs[:, t, :], in0=xs[:, t, :], scalar=x2_rms[:, t:t + 1], in1=final_row[:, :], op0=ALU.mult, op1=ALU.mult)\
                    .then_inc(out_ready, 1)

            dve.wait_ge(final_in, 16)
            dve.wait_ge(v_added, NSEL + 1)
            for t in range(NT):
                if t == SPARSE:
                    link(tt(y[:, t, :], y[:, t, :], gate2, ALU.mult))
                else:
                    dve.wait_ge(v_used, NKEYS)
                    for s in range(2):
                        cols = slice(s * HALF, (s + 1) * HALF)
                        ins = tt(y[:, t, cols], bank[2 + 2 * ORDER.index(t) + s][:, :], gate2[:, cols], ALU.mult)
                    link(ins)
                tt(xs[:, t, :], xs[:, t, :], y[:, t, :], ALU.add).then_inc(x2_ready, 1)
                if t:
                    finish(t - 1)
            finish(NT - 1)


def kernel(x, c, w_ada, b_ada, norm1_g, w_in, b_f, sg_ln_g, sg_ln_b, sg_w, sg_b, out_g_sg, out_g_fox,
           w_out, norm2_g, w_query, sub_keys, expert_u, expert_v, final_g):
    import concourse.bacc as bacc
    import numpy as np
    from concourse.bass_utils import run_bass_kernel_spmd

    laid_out = {
        "x": x[0], "cT": np.transpose(c.reshape(KC, P)), "w_ada": w_ada[0], "b_ada": b_ada[0], "norm1_g": norm1_g[0], "w_in": w_in[0],
        "b_f": b_f[0], "sg_ln_g": sg_ln_g[0], "sg_ln_b": sg_ln_b[0],
        "sg_wT": np.transpose(sg_w[0], (2, 0, 1)),
        "sg_bT": np.transpose(sg_b[0]),
        "out_gT": np.transpose(np.concatenate([out_g_sg[0], out_g_fox[0]]).reshape(KC, P)), "w_out": w_out[0], "norm2_g": norm2_g[0],
        "w_query": w_query[0],
        "sub_keysT": np.transpose(sub_keys[0].reshape(HP, NKEYS, P), (2, 0, 1)),
        "uT": np.transpose(expert_u[0].reshape(NKEYS, NKEYS, KC, P), (0, 3, 2, 1)).reshape(NKEYS, P, D),
        "expert_u": expert_u[0], "expert_v": expert_v[0], "final_g": final_g,
    }
    nc = bacc.Bacc("TRN2", target_bir_lowering=False, num_devices=1)
    arrays, args = {}, []
    for name, a in laid_out.items():
        a = np.ascontiguousarray(a)
        arrays[f"in_{name}"] = a
        args.append(nc.dram_tensor(f"in_{name}", a.shape, mybir.dt.from_np(a.dtype), kind="ExternalInput").ap())
    args.append(nc.dram_tensor("out", (SEQ, D), F32, kind="ExternalOutput").ap())
    program(nc, *args)
    result = run_bass_kernel_spmd(nc, [arrays], core_ids=[0])
    return result.results[0]["out"].reshape(1, SEQ, D)
```

```python
from contextlib import ExitStack

import concourse.bass as bass
from concourse import mybir

F32 = mybir.dt.float32
F32R = mybir.dt.float32r
U32 = mybir.dt.uint32
ALU = mybir.AluOpType
ACT = mybir.ActivationFunctionType
AX_X = mybir.AxisListType.X

P = 128
SEQ = 512
D = 1024
NT = SEQ // P
KC = D // P
HALF = 512
HEADS = 8
DH = 64
PH = 8
HP = 2 * PH
NKEYS = 128
TOPK = 16
NSEL = PH * TOPK
N_EXPERTS = NKEYS * NKEYS
EPS = 1e-6
MASKED = -1e30
TAKEN = -3e38

SPARSE = 0
ORDER = (1, 2, 3, SPARSE)
DENSE = NT - 1
DTOK = DENSE * P
ROWS = 8
RAW = 4
STEP_ROWS = 2
STAGED = 8
GROUP = 32
GROUPS = DTOK // GROUP
BATCH = 4
BATCHES = P // BATCH
HOT = 4
AHEAD = 8
BODY = 8
ITERS = NKEYS // BODY
GLOAD = 4
SLOTS = 6
ADA_EARLY = [("ada", g) for g in range(4)]
W_IN = [("w_in", c) for c in ("zv", "v", "zu", "q", "k")]
ADA_LATE = [("ada", g) for g in range(4, 12)]
RESIDENT = [("w_query", 0), ("w_out", 0), ("w_out", 1)] + [("w_query", g) for g in range(1, 4)]
STREAM = ADA_EARLY + W_IN + ADA_LATE + RESIDENT
W_IN_COL = {"zu": 0, "zv": 512, "q": 1024, "k": 1536, "v": 2048}
F_COL = 2560

QUERY_PAIRS = ((0, 1), (2, 3))

ATTN = [(qt, h) for qt in range(NT) for h in range(HEADS)]


def plan_banks():
    jobs = [(("ada", g), 4 + g % 2) for g in range(4)]
    jobs += [(("h1T", t, s), 6 + s) for t in range(NT) for s in range(2)]
    proj = [("zv", t) for t in range(NT)] + [("v", t) for t in range(NT)] + [("f",)]
    proj += [("zu", t) for t in range(NT)] + [("q", c) for c in range(4)] + [("k", c) for c in range(4)]
    jobs += [(j, n % 4) for n, j in enumerate(proj)]
    jobs += [(("ada", g), 4 + g % 2) for g in range(4, 12)]
    jobs += [(("cum",), 6)]
    jobs += [(("sgu", b), b) for b in range(4)]
    jobs += [(("S", n), 4 + n % 2) for n in range(len(ATTN))]
    jobs += [(("PT", n), 6 + n % 2) for n in range(len(ATTN))]
    jobs += [(("O", t), t % 2) for t in range(NT)]
    jobs += [(("yT", t, s), (2, 6)[t % 2] + s) for t in range(NT) for s in range(2)]
    jobs += [(("mix", t, s), (0, 4)[t % 2] + s) for t in ORDER for s in range(2)]
    def h2T_jobs(t):
        return [(("h2T", t, s), (2, 6)[t % 2] + s) for s in range(2)]

    jobs += h2T_jobs(ORDER[0])
    for n in range(NT):
        for pair in QUERY_PAIRS:
            jobs += [(("qrow", n, g), (4, 5, 0, 1)[g]) for g in pair]
            jobs += [(("qT", n, g), (2, 3, 4, 5)[g]) for g in pair]
            jobs += [(("score", n, g), g) for g in pair]
        if n == 0:
            for t in ORDER[1:]:
                jobs += h2T_jobs(t)
        else:
            jobs += [(("turn", n - 1), 6)]
    place, count = {}, [0] * 8
    for name, b in jobs:
        count[b] += 1
        place[name] = (b, count[b])
    return place


def program(nc, x, cT, w_ada, b_ada, norm1_g, w_in, b_f, sg_ln_g, sg_ln_b, sg_wT, sg_bT,
            out_gT, w_out, norm2_g, w_query, sub_keysT, uT, expert_u, expert_v, final_g, out):
    place = plan_banks()
    slot_of = {name: n % SLOTS for n, name in enumerate(STREAM)}
    load_of = {name: 16 * (n // SLOTS + 1) for n, name in enumerate(STREAM)}

    with ExitStack() as ctx:
        def sb(name, shape, dt=F32):
            return ctx.enter_context(nc.sbuf_tensor(name, shape, dt))

        def sem(name):
            return ctx.enter_context(nc.semaphore(name))

        def aligned(offset):
            return (offset + 31) // 32 * 32

        weights_at = aligned(nc.sbuf_base)
        weights = sb("weights", [P, SLOTS, KC, HALF])
        shared_at = aligned(nc.sbuf_base)
        shared = sb("shared", [P, 8 * D])
        xs = sb("xs", [P, NT, D])
        ada = sb("ada", [P, 6 * D])
        hT = sb("hT", [P, KC, SEQ])
        y_at = aligned(nc.sbuf_base)
        y = sb("y", [P, NT, D])
        ident = sb("ident", [P, P])
        final_row = sb("final_row", [P, D])
        idx = sb("idx", [P, 2, NSEL], U32)
        gate = sb("gate", [P, NSEL])
        act_w = sb("act_w", [P, NSEL])
        misc = sb("misc", [P, 160])
        idx_slot = sb("idx_slot", [P, 2, STAGED], U32)

        h1 = shared[:, 0:4 * D].rearrange("p (t d) -> p t d", t=NT)
        q_z = shared[:, 0:4 * D].rearrange("p (h s) -> p h s", h=HEADS)
        kT = shared[:, 4 * D:6 * D].rearrange("p (c s) -> p c s", c=4)
        v_tok = shared[:, 6 * D:8 * D].rearrange("p (t d) -> p t d", t=NT)

        hTf = hT[:, :, :].rearrange("p k s -> p (k s)")
        norm1_row = hTf[:, 0:D]
        sgw = hTf[:, 0:D].rearrange("p (h t) -> p h t", h=HEADS)
        p_exp = hTf[:, D:2 * D].rearrange("p (b s) -> p b s", b=2)
        p_T = hTf[:, 2 * D:3 * D].rearrange("p (b s) -> p b s", b=2)
        ncum = hTf[0:HEADS, 3 * D:3 * D + SEQ]
        causal = hTf[:, 3 * D + SEQ:3 * D + SEQ + P]
        squares = shared[:, 0:4 * D].rearrange("p (t d) -> p t d", t=NT)
        yT = shared[:, 4 * D:8 * D].rearrange("p (t k n) -> p t k n", t=NT, k=KC)
        h2T_sparse = final_row[:, :].rearrange("p (k t) -> p k t", k=KC)

        def h2T(t):
            return h2T_sparse if t == SPARSE else y[:, t, :].rearrange("p (k t) -> p k t", k=KC)

        def scratch(n):
            return (shared, hTf)[n % 2]

        def qT(n):
            return scratch(n)[:, 0:2 * D].rearrange("p (g t) -> p g t", g=HP)

        def cand_of(n):
            return scratch(n)[:, 0:2 * D].rearrange("p (h e) -> p h e", h=PH)

        def qrow(n):
            return scratch(n)[:, 2 * D:4 * D]

        def scores(n):
            return scratch(n)[:, 2 * D:4 * D].rearrange("p (g n) -> p g n", g=HP)

        def picks(n):
            return [scratch(n)[:, 2 * D + j * NSEL:2 * D + (j + 1) * NSEL] for j in range(5)]

        PICKS = [(s, hh) for s in range(2) for hh in range(2)]

        def onehot(n, c):
            whole = row(3) if c == 2 else scratch(n)[:, c % 3 * D:(c % 3 + 1) * D]
            return whole.rearrange("p (s a) -> p s a", a=TOPK)

        hot_j = shared[:, 4 * D:6 * D].rearrange("p (b t j) -> p b t j", b=HOT, t=BATCH)
        hot_i = shared[:, 6 * D:8 * D].rearrange("p (b t i) -> p b t i", b=HOT, t=BATCH)

        def slot(n):
            return weights[:, n, :, :].rearrange("p k n -> p (k n)")

        def slot_f32r(name, n, first, shape):
            return nc.alloc_sbuf_tensor_at(name, shape, F32R, offset=weights_at + 4 * (n * KC * HALF + first))

        def shared_f32r(name, first, shape):
            return nc.alloc_sbuf_tensor_at(name, shape, F32R, offset=shared_at + 4 * first)

        def ring(r):
            return (hTf if r < ROWS // 2 else slot(1))[:, r % (ROWS // 2) * D:(r % (ROWS // 2) + 1) * D]

        staging = [slot(b).rearrange("p (i t) -> p i t", t=GROUP) for b in range(2)]
        u_raw = slot(2).rearrange("p (b n) -> p b n", b=RAW)
        u_lo = slot_f32r("u_lo", 2, 0, [P, RAW, D])
        u_hi = [slot_f32r(f"u_hi{b}", n, 3 * D, [P, D]) for b, n in enumerate((3, 5))]
        ahead = slot(3)[:, 0:AHEAD * DTOK].rearrange("p (b n) -> p b n", b=AHEAD)
        v_raw = slot(4).rearrange("p (b n) -> p b n", b=RAW)
        v_lo = slot_f32r("v_lo", 4, 0, [P, RAW, D])
        v_hi = shared_f32r("v_hi", 6 * D, [P, 2, D])
        g_block = slot(5)[:, 0:2 * GLOAD * DTOK].rearrange("p (b g i t) -> p b g i t", b=2, g=GROUPS, i=GLOAD)
        w_raw = slot(0)[:, 0:2 * DTOK].rearrange("p (b n) -> p b n", b=2)
        w_lo = slot_f32r("w_lo", 0, 0, [P, 2, DTOK])
        w_hi = slot_f32r("w_hi", 0, 2 * DTOK, [P, 2, DTOK])
        h2_hi = shared_f32r("h2_hi", 0, [P, DENSE, KC, P])
        h2_lo = nc.alloc_sbuf_tensor_at("h2_lo", [P, DENSE, KC, P], F32R, offset=y_at + 4 * D)
        g_dram = nc.dram_tensor("gates_dense", (GROUPS, P, NKEYS * GROUP), F32).ap()

        def row(n):
            return ada[:, n * D:(n + 1) * D]
        shift1, scale1, gate1, shift2, scale2, gate2 = (row(n) for n in range(6))
        ln_g, ln_b = ada[:, 0:HALF], ada[:, HALF:D]
        v_sq = ada[:, D:2 * D]
        norm2_row = ada[:, D:2 * D]
        keysT = ada[:, 0:2 * D].rearrange("p (g n) -> p g n", g=HP)
        top_v = row(4)[:, 0:256].rearrange("p (g k) -> p g k", g=HP)
        top_i = row(4)[:, 256:512].bitcast(U32).rearrange("p (g k) -> p g k", g=HP)
        top_f = row(4)[:, 512:768].rearrange("p (g k) -> p g k", g=HP)
        best_v = row(4)[:, 768:896].rearrange("p (h k) -> p h k", h=PH)
        best_p = row(4)[:, 896:1024].bitcast(U32).rearrange("p (h k) -> p h k", h=PH)
        turned = ada[:, 2 * D:2 * D + 6 * P].rearrange("p (b c t) -> p b c t", b=2, c=3)
        iota128 = ada[:, 2 * D + 6 * P:2 * D + 7 * P]

        tri = act_w[:, :]
        c_col, c_act, c_exp = misc[:, 0:8], misc[:, 8:16], misc[:, 16:24]
        out_g = misc[:, 24:32]
        sgb = misc[:, 32:40]
        bf_row = misc[:, 40:48]
        iota16 = misc[:, 48:64]
        x_ss, x_rms = misc[:, 64:68], misc[:, 68:72]
        y_var = act_w[:, 0:64].rearrange("p (t h) -> p t h", t=NT)
        y_rms = act_w[:, 64:128].rearrange("p (t h) -> p t h", t=NT)
        g_now = misc[:, 128:128 + HOT * BATCH]
        x1_ss, x1_rms = misc[:, 104:108], misc[:, 116:120]
        x2_ss, x2_rms = misc[:, 120:124], misc[:, 124:128]
        gate_sum = misc[:, 108:116]
        logit = idx[:, 0, 0:32].bitcast(F32)
        lsg_e = idx[:, 0, 32:64].bitcast(F32)
        lsg = idx[:, 0, 64:96].bitcast(F32)
        nmax = idx[:, 0, 96:128].bitcast(F32)
        rsum = idx[:, 1, 0:32].bitcast(F32)
        v_mean = idx[:, 1, 32:64].bitcast(F32)
        v_var = idx[:, 1, 64:96].bitcast(F32)
        o_scale = idx[:, 1, 96:128].bitcast(F32)
        f_w = gate[:, 0:64].rearrange("p (k f) -> p k f", k=KC)
        iota128_u = idx[:, 1, :]
        iota_u = gate[:, 64:80].bitcast(U32)
        ones = gate[:, 80:81].broadcast_to([P, P])

        bank = [ctx.enter_context(nc.psum_tensor(f"bank{b}", [P, HALF], F32)) for b in range(8)]

        weight_in = [sem(f"weight_in{s}") for s in range(SLOTS)]
        full = [sem(f"bank{b}_full") for b in range(8)]
        read = [sem(f"bank{b}_read") for b in range(8)]
        gathered = [sem(f"gathered{r}") for r in range(ROWS)]
        g_stored = [sem(f"g_stored{b}") for b in range(2)]
        g_in = [sem(f"g_in{b}") for b in range(2)]
        u_in = [sem(f"u_in{b}") for b in range(RAW)]
        v_in = [sem(f"v_in{b}") for b in range(RAW)]
        x_in, c_in, small_in, norm1_in = sem("x_in"), sem("c_in"), sem("small_in"), sem("norm1_in")
        ada_zeroed, b_ada_early, b_ada_late = sem("ada_zeroed"), sem("b_ada_early"), sem("b_ada_late")
        norm2_in, ln_in, sgw_in = sem("norm2_in"), sem("ln_in"), sem("sgw_in")
        final_in, fw_in, keys_in, stored = sem("final_in"), sem("fw_in"), sem("keys_in"), sem("stored")
        made, causal_made, sgw_masked, qz_zero = sem("made"), sem("causal_made"), sem("sgw_masked"), sem("qz_zero")
        c_exped = sem("c_exped")
        ada_summed = sem("ada_summed")
        a1_done, a2_done, h1_ready = sem("a1_done"), sem("a2_done"), sem("h1_ready")
        x_squared, x_mean, x_root = sem("x_squared"), sem("x_mean"), sem("x_root")
        f_abs, f_exp, f_plus, f_log, f_done = sem("f_abs"), sem("f_exp"), sem("f_plus"), sem("f_log"), sem("f_done")
        v_var_ready, v_root, v_norm = sem("v_var_ready"), sem("v_root"), sem("v_norm")
        neg_max, pT_used = sem("neg_max"), sem("pT_used")
        w_out_gated = sem("w_out_gated")
        y_squared, y_mean, y_root, y_ready = sem("y_squared"), sem("y_mean"), sem("y_root"), sem("y_ready")
        x1_squared, x1_mean, x1_root, h2_ready = sem("x1_squared"), sem("x1_mean"), sem("x1_root"), sem("h2_ready")
        best_ready, gate_exp, topk_done = sem("best_ready"), sem("gate_exp"), sem("topk_done")
        granted, idx_staged = sem("slot_granted"), sem("idx_staged")
        dot_done, gelu_done, w_ready = sem("dot_done"), sem("gelu_done"), sem("w_ready")
        v_added = sem("v_added")
        g_staged, hot_granted = sem("g_staged"), sem("hot_granted")
        picks_marked, picks_weighted = sem("picks_marked"), sem("picks_weighted")
        gates_ready, iota_made = sem("gates_ready"), sem("iota_made")
        hot_made, hot_gated, built = sem("hot_made"), sem("hot_gated"), sem("built")
        build_granted, build_read = sem("build_granted"), sem("build_read")
        h2_hi_made, h2_lo_made = sem("h2_hi_made"), sem("h2_lo_made")
        u_hi_made, u_lo_made, v_hi_made, v_lo_made = sem("u_hi_made"), sem("u_lo_made"), sem("v_hi_made"), sem("v_lo_made")
        w_made, w_hi_made, w_lo_made = sem("w_made"), sem("w_hi_made"), sem("w_lo_made")
        a_full, a_read = sem("a_full"), sem("a_read")
        v_used = sem("v_used")
        x2_ready, x2_squared, x2_mean, x2_root = sem("x2_ready"), sem("x2_squared"), sem("x2_mean"), sem("x2_root")
        out_ready = sem("out_ready")
        v_chain, g_chain = sem("vector_chain"), sem("gpsimd_chain")

        block = ctx.enter_context(nc.Block())

        def wait_full(eng, *name):
            b, n = place[name]
            eng.wait_ge(full[b], n)
            return bank[b]

        def wait_read(eng, *name):
            b, n = place[name]
            eng.wait_ge(read[b], n)

        def release(ins, *name):
            ins.then_inc(read[place[name][0]], 1)

        def group_source(kind, g):
            if kind == "ada":
                src = w_ada[:, g * HALF:(g + 1) * HALF]
            elif kind == "w_in":
                src = w_in[:, W_IN_COL[g]:W_IN_COL[g] + HALF]
            elif kind == "w_out":
                src = w_out[:, g * HALF:(g + 1) * HALF]
            else:
                src = w_query[:, g * HALF:(g + 1) * HALF]
            return src.rearrange("(k p) n -> p k n", p=P)

        def one_row(v):
            return v.rearrange("(a n) -> a n", a=1)

        def on_all(v):
            return one_row(v).broadcast_to([P, v.shape[0]])

        def wait_weights(eng, *name):
            eng.wait_ge(weight_in[slot_of[name]], load_of[name])
            return weights[:, slot_of[name], :, :]

        @block.sync
        def _(sp):
            def load_group(n):
                name = STREAM[n]
                if n >= SLOTS:
                    kind, g = STREAM[n - SLOTS]
                    if kind == "ada":
                        sp.wait_ge(ada_summed, g + 1)
                    else:
                        wait_full(sp, g, 3)
                sp.dma_start(weights[:, slot_of[name], :, :], group_source(*name)).then_inc(weight_in[slot_of[name]], 16)

            sp.dma_start(c_col, cT).then_inc(c_in, 16)
            load_group(0)
            load_group(1)
            sp.wait_ge(weight_in[0], 16)
            load_group(2)
            sp.wait_ge(weight_in[1], 16)
            load_group(3)
            sp.wait_ge(weight_in[2], 16)
            sp.dma_start(xs[:, :, :], x.rearrange("(t p) d -> p t d", p=P)).then_inc(x_in, 16)
            sp.dma_start(norm1_row, on_all(norm1_g)).then_inc(norm1_in, 16)
            sp.wait_ge(weight_in[3], 16)
            for n in range(4, SLOTS):
                load_group(n)
            sp.wait_ge(made, 3)
            sp.dma_start(f_w, w_in[:, F_COL:F_COL + HEADS].rearrange("(k p) n -> p k n", p=P)).then_inc(fw_in, 16)
            sp.dma_start(bf_row, on_all(b_f)).then_inc(small_in, 16)
            sp.dma_start(sgb, sg_bT).then_inc(small_in, 16)
            sp.dma_start(out_g, out_gT).then_inc(small_in, 16)
            for n in range(SLOTS, SLOTS + 3):
                load_group(n)
            sp.wait_ge(h1_ready, NT)
            sp.dma_start(ln_g, on_all(sg_ln_g)).then_inc(ln_in, 16)
            sp.dma_start(ln_b, on_all(sg_ln_b)).then_inc(ln_in, 16)
            for n in range(SLOTS + 3, len(STREAM)):
                load_group(n)
                if STREAM[n] == ("ada", 9):
                    sp.wait_ge(v_var_ready, 1)
                    sp.dma_start(norm2_row, on_all(norm2_g)).then_inc(norm2_in, 16)
                    wait_full(sp, "k", 3)
                    sp.dma_start(sgw, sg_wT).then_inc(sgw_in, 16)
            sp.wait_ge(a2_done, 1)
            sp.dma_start(keysT, sub_keysT).then_inc(keys_in, 16)

            def store_groups(first, last):
                for g in range(first, last):
                    sp.wait_ge(build_read, (g + 1) * GROUP // BATCH)
                    sp.dma_start(g_dram[g], staging[g % 2].rearrange("p i t -> p (i t)")).then_inc(g_stored[g % 2], 16)

            def load_u(I, r):
                sp.dma_start(u_raw[:, r % RAW, :], uT[bass.ds(BODY * I + r, 1)].rearrange("b p n -> p (b n)"))\
                    .then_inc(u_in[r % RAW], 16)

            def load_v(I, r):
                sp.dma_start(v_raw[:, r % RAW, :], expert_v[bass.ds((BODY * I + r) * P, P), :]).then_inc(v_in[r % RAW], 16)

            def load_g(I, half):
                src = g_dram[:, :, bass.ds((BODY * I + GLOAD * half) * GROUP, GLOAD * GROUP)]
                sp.dma_start(g_block[:, half].rearrange("p g i t -> p g (i t)"), src.rearrange("g p n -> p g n"))\
                    .then_inc(g_in[half], 16)

            store_groups(0, 2 * GROUPS // DENSE)
            for g in range(4):
                wait_full(sp, "qrow", NT - 1, g)
            for n in range(RAW):
                load_u(0, n)
            sp.dma_start(final_row[:, :], on_all(final_g)).then_inc(final_in, 16)
            store_groups(2 * GROUPS // DENSE, GROUPS)
            for b in range(2):
                sp.wait_ge(g_stored[b], 16 * GROUPS // 2)
            load_g(0, 0)
            for n in range(RAW, AHEAD):
                sp.wait_ge(a_full, n - RAW + 1)
                load_u(0, n)

            def step(I, r, more, first):
                m = BODY * I + r
                if more:
                    sp.wait_ge(a_full, m + AHEAD - RAW + 1)
                    load_u(I + 1, r)
                if not (first and r < RAW):
                    sp.wait_ge(v_used, m - RAW + 1)
                load_v(I, r)
                if r == 0:
                    if not first:
                        sp.wait_ge(w_made, m)
                    load_g(I, 1)
                if r == GLOAD and more:
                    sp.wait_ge(w_made, m)
                    load_g(I + 1, 0)

            for r in range(BODY):
                step(0, r, True, True)
            with sp.Fori(1, ITERS - 1) as I:
                for r in range(BODY):
                    step(I, r, True, False)
            for r in range(BODY):
                step(ITERS - 1, r, False, False)
            for t in range(NT):
                sp.wait_ge(out_ready, t + 1)
                sp.dma_start(out[t * P:(t + 1) * P, :], xs[:, t, :]).then_inc(stored, 16)
            sp.wait_ge(stored, 16 * NT)

        @block.gpsimd
        def _(pool):
            links = [0]

            def link(ins):
                links[0] += 1
                ins.then_inc(g_chain, 1)
                pool.wait_ge(g_chain, links[0])

            nc.gpsimd.memset(ada[:, 0:4 * HALF], 0.0).then_inc(ada_zeroed, 1)
            nc.gpsimd.memset(ada[:, 4 * HALF:6 * D], 0.0).then_inc(ada_zeroed, 1)
            link(nc.gpsimd.memset(ident[:, :], 0.0))
            link(nc.gpsimd.memset(gate[:, :], 1.0))
            link(nc.gpsimd.memset(tri, 1.0))
            nc.gpsimd.iota(iota_u, [[1, TOPK]], base=0, channel_multiplier=0).then_inc(made, 1)
            nc.gpsimd.affine_select(out=ident[:, :], in_=ident[:, :], compare_op=ALU.not_equal, fill=1.0,
                                    base=0, pattern=[[-1, P]], channel_multiplier=1).then_inc(made, 1)
            nc.gpsimd.affine_select(out=tri, in_=tri, compare_op=ALU.is_ge, fill=0.0,
                                    base=0, pattern=[[1, P]], channel_multiplier=-1).then_inc(made, 1)
            wait_full(pool, "h1T", 3, 1)
            nc.gpsimd.memset(q_z, 0.0).then_inc(qz_zero, 1)
            wait_full(pool, "k", 3)
            link(nc.gpsimd.memset(causal, 0.0))
            nc.gpsimd.affine_select(out=causal, in_=causal, compare_op=ALU.is_ge, fill=MASKED,
                                    base=0, pattern=[[-1, P]], channel_multiplier=1).then_inc(causal_made, 1)
            pool.wait_ge(sgw_in, 16)
            nc.gpsimd.affine_select(out=sgw, in_=sgw, compare_op=ALU.is_ge, fill=0.0,
                                    base=0, pattern=[[0, HEADS], [1, P]], channel_multiplier=-1).then_inc(sgw_masked, 1)
            wait_read(pool, "ada", 4)
            wait_read(pool, "ada", 5)
            for g in range(2):
                w = wait_weights(pool, "w_out", g)
                for k in range(KC):
                    nc.gpsimd.tensor_tensor(w[:, k, :], w[:, k, :], gate1[:, g * HALF:(g + 1) * HALF],
                                            ALU.mult).then_inc(w_out_gated, 1)

            wait_read(pool, "O", NT - 1)
            nc.gpsimd.iota(iota128_u, [[1, P]], base=0, channel_multiplier=0).then_inc(iota_made, 1)
            pool.wait_ge(iota_made, 1)
            pool.wait_ge(w_out_gated, 2 * KC)
            nc.gpsimd.tensor_copy(iota128, iota128_u).then_inc(iota_made, 1)
            pool.wait_ge(iota_made, 2)

            def gate_hot_rows(n, i, first):
                if not first:
                    pool.wait_ge(hot_gated, n * BATCHES + HOT * i)
                nc.gpsimd.tensor_copy(g_now, turned[:, n % 2, 2, bass.ds(HOT * BATCH * i, HOT * BATCH)]).then_inc(g_staged, 1)
                pool.wait_ge(g_staged, n * BATCHES // HOT + i + 1)
                pool.sem_inc(hot_granted, 1)
                for b in range(HOT):
                    pool.wait_ge(hot_made, n * BATCHES + HOT * i + b + 1)
                    nc.gpsimd.tensor_tensor(hot_i[:, b], hot_i[:, b],
                                            g_now[:, b * BATCH:(b + 1) * BATCH].unsqueeze(2).broadcast_to([P, BATCH, P]), ALU.mult)\
                        .then_inc(hot_gated, 1)

            def weight_picks(n):
                for c, (s, hh) in enumerate(PICKS):
                    pool.wait_ge(picks_marked, len(PICKS) * n + c + 1)
                    oh = onehot(n, c).rearrange("p (h k) a -> p h k a", h=4)
                    numbers = top_f.rearrange("p (h s) k -> p h s k", s=2)[:, 4 * hh:4 * hh + 4, s, :]
                    nc.gpsimd.tensor_tensor(oh, oh, numbers.unsqueeze(2).broadcast_to([P, 4, TOPK, TOPK]), ALU.mult)\
                        .then_inc(picks_weighted, 1)

            for n in range(DENSE):
                weight_picks(n)
                wait_read(pool, "turn", n)
                if n == 0:
                    gate_hot_rows(n, 0, True)
                with pool.Fori(1 if n == 0 else 0, BATCHES // HOT) as i:
                    gate_hot_rows(n, i, False)

            def gather_rows(table, which, used):
                def one_round(i, half, first):
                    nc.gpsimd.tensor_copy(idx_slot[:, half, :], idx[:, 0, bass.ds((2 * i + half) * STAGED, STAGED)])\
                        .then_inc(idx_staged, 1)
                    pool.wait_ge(idx_staged, which * NSEL // STAGED + 2 * i + half + 1)
                    for r in range(STAGED):
                        if first and r < ROWS:
                            if which:
                                pool.wait_ge(dot_done, NSEL - ROWS + r + 1)
                        else:
                            pool.wait_ge(used, (2 * i + half) * STAGED + r - ROWS + 1 + which)
                        pool.sem_inc(granted, 1)
                        nc.gpsimd.indirect_dma_start(ring(r % ROWS), None, table,
                                                     bass.IndirectOffsetOnAxis(idx_slot[:, half, r:r + 1], 0))\
                            .then_inc(gathered[r % ROWS], 16)

                one_round(0, 0, True)
                one_round(0, 1, False)
                with pool.Fori(1, NSEL // STAGED // 2) as i:
                    one_round(i, 0, False)
                    one_round(i, 1, False)

            weight_picks(NT - 1)
            pool.wait_ge(g_stored[1], 16 * GROUPS // 2)
            pool.wait_ge(topk_done, 1)
            gather_rows(expert_u, 0, dot_done)
            gather_rows(expert_v, 1, v_added)

        @block.scalar
        def _(act):
            def load_b_ada(first, last, signal):
                for g in range(first, last):
                    cols = slice(g * HALF, (g + 1) * HALF)
                    act.dma_start(ada[0:1, cols], one_row(b_ada[cols])).then_inc(signal, 16)

            act.wait_ge(ada_zeroed, 1)
            load_b_ada(0, 4, b_ada_early)
            act.wait_ge(c_in, 16)
            nc.scalar.activation(c_exp, c_col, ACT.Exp, scale=-1.0).then_inc(c_exped, 1)
            act.wait_ge(x_in, 16)
            for t in range(NT):
                nc.scalar.activation(y[:, t, :], xs[:, t, :], ACT.Square, accum_out=x_ss[:, t:t + 1]).then_inc(x_squared, 1)
            act.wait_ge(ada_zeroed, 2)
            load_b_ada(4, 12, b_ada_late)
            act.wait_ge(x_mean, 1)
            nc.scalar.activation(x_rms, x_ss, ACT.Sqrt).then_inc(x_root, 1)

            def ada_row(g):
                b = wait_full(act, "ada", g)
                release(nc.scalar.activation(ada[:, g * HALF:(g + 1) * HALF], b[:, :], ACT.Copy), "ada", g)

            def copy_chunks(dst, name, func=ACT.Copy):
                b = wait_full(act, *name)
                release(nc.scalar.activation(dst, b[:, :].rearrange("p (k t) -> p k t", k=4), func), *name)

            for g in range(4):
                ada_row(g)
            act.wait_ge(a1_done, 1)
            for t in range(NT):
                for s in range(2):
                    copy_chunks(hT[:, 4 * s:4 * s + 4, t * P:(t + 1) * P], ("h1T", t, s))
            for t in range(NT):
                b = wait_full(act, "zv", t)
                release(nc.scalar.activation(y[:, t, HALF:D], b[:, :], ACT.Gelu), "zv", t)
            act.wait_ge(f_abs, 1)
            nc.scalar.activation(lsg_e, lsg_e, ACT.Exp, scale=-1.0).then_inc(f_exp, 1)
            act.wait_ge(f_plus, 1)
            nc.scalar.activation(lsg_e, lsg_e, ACT.Ln).then_inc(f_log, 1)
            for t in range(NT):
                b = wait_full(act, "zu", t)
                release(nc.scalar.activation(y[:, t, 0:HALF], b[:, :], ACT.Gelu), "zu", t)
            act.wait_ge(qz_zero, 1)
            for n in range(4):
                b = wait_full(act, "q", n)
                nc.scalar.activation(q_z[0:DH, 2 * n, :], b[0:DH, :], ACT.Copy, scale=DH ** -0.5)
                release(nc.scalar.activation(q_z[DH:P, 2 * n + 1, :], b[DH:P, :], ACT.Copy, scale=DH ** -0.5), "q", n)
            act.wait_ge(v_var_ready, 1)
            nc.scalar.activation(v_var, v_var, ACT.Sqrt).then_inc(v_root, 1)
            for g in range(4, 12):
                ada_row(g)
            b = wait_full(act, "cum")
            release(nc.scalar.activation(ncum, b[0:HEADS, :], ACT.Copy, scale=-1.0), "cum")

            for n, (qt, h) in enumerate(ATTN):
                keys = (qt + 1) * P
                act.wait_ge(neg_max, n + 1)
                if n >= 2:
                    wait_full(act, "PT", n - 2)
                release(nc.scalar.activation(p_exp[:, n % 2, 0:keys], bank[place["S", n][0]][:, 0:keys], ACT.Exp,
                                             bias=nmax[:, n:n + 1], accum_out=rsum[:, n:n + 1]),
                        "S", n)

            wait_read(act, "O", NT - 1)
            for t in range(NT):
                nc.scalar.activation(squares[:, t, :], y[:, t, :], ACT.Square).then_inc(y_squared, 1)
            for t in range(NT):
                act.wait_ge(y_mean, t + 1)
                nc.scalar.activation(y_rms[:, t], y_var[:, t], ACT.Sqrt).then_inc(y_root, 1)

            def x1_roots(n):
                t = ORDER[n]
                act.wait_ge(x1_mean, n + 1)
                nc.scalar.activation(x1_rms[:, t:t + 1], x1_ss[:, t:t + 1], ACT.Sqrt).then_inc(x1_root, 1)

            for n, t in enumerate(ORDER):
                wait_read(act, "mix", t, 0)
                wait_read(act, "mix", t, 1)
                nc.scalar.activation(squares[:, t, :], xs[:, t, :], ACT.Square, accum_out=x1_ss[:, t:t + 1]).then_inc(x1_squared, 1)
                if n:
                    x1_roots(n - 1)
            x1_roots(NT - 1)

            def h2_turned(t):
                wait_full(act, "h2T", t, 1)
                for s in range(2):
                    copy_chunks(h2T(t)[:, 4 * s:4 * s + 4, :], ("h2T", t, s))

            def query(n):
                if n >= 2:
                    wait_full(act, "turn", n - 2)
                for pair in QUERY_PAIRS:
                    for g in pair:
                        b = wait_full(act, "qrow", n, g)
                        release(nc.scalar.activation(qrow(n)[:, g * HALF:(g + 1) * HALF], b[:, :], ACT.Copy), "qrow", n, g)
                    for g in pair:
                        copy_chunks(qT(n)[:, 4 * g:4 * g + 4, :], ("qT", n, g))
                    for g in pair:
                        copy_chunks(scores(n)[:, 4 * g:4 * g + 4, :], ("score", n, g))

            def gate_exps(n):
                act.wait_ge(best_ready, n + 1)
                nc.scalar.activation(gate[:, :], gate[:, :], ACT.Exp).then_inc(gate_exp, 1)

            def round_u(I, r, first=False):
                act.wait_ge(u_in[r % RAW], 16 * (BODY // RAW * I + r // RAW + 1))
                if not (first and r < 2):
                    act.wait_ge(a_full, BODY * I + r - 1)
                nc.scalar.activation(u_hi[r % 2][:, :], u_raw[:, r % RAW, :], ACT.Copy).then_inc(u_hi_made, 1)

            def round_h2():
                for d in range(DENSE):
                    wait_read(act, "h2T", ORDER[d], 0)
                    wait_read(act, "h2T", ORDER[d], 1)
                    nc.scalar.activation(h2_hi[:, d], h2T(ORDER[d]), ACT.Copy).then_inc(h2_hi_made, 1)

            def build(n):
                if n >= 2:
                    act.wait_ge(build_read, (n - 1) * BATCHES)
                b = wait_full(act, "turn", n)
                release(nc.scalar.activation(turned[:, n % 2], b[:, 0:3 * P].rearrange("p (c t) -> p c t", c=3), ACT.Copy), "turn", n)
                if n == DENSE - 1:
                    round_h2()
                    for r in range(2):
                        round_u(0, r, True)
                per_group = GROUP // BATCH
                for g in range(P // GROUP):
                    group = n * P // GROUP + g
                    if group >= 2:
                        act.wait_ge(g_stored[group % 2], 16 * (group // 2))
                    with act.Fori(0, per_group // HOT) as i:
                        for b in range(HOT):
                            act.wait_ge(built, group * per_group + HOT * i + b + 1)
                            act.sem_inc(build_granted, 1)
                            out_t = staging[group % 2][:, :, bass.ds((HOT * i + b) * BATCH, BATCH)]
                            nc.scalar.activation(out_t, bank[6 + b % 2][:, :].rearrange("p (t i) -> p i t", t=BATCH), ACT.Copy)\
                                .then_inc(build_read, 1)

            h2_turned(ORDER[0])
            query(0)
            for t in ORDER[1:]:
                h2_turned(t)
            for n in range(DENSE):
                query(n + 1)
                gate_exps(n)
                build(n)

            def gelu(I, r):
                act.wait_ge(a_full, BODY * I + r + 1)
                nc.scalar.activation(ahead[:, r, :], bank[r % 2][:, 0:DTOK], ACT.Gelu).then_inc(a_read, 1)

            for n in range(AHEAD):
                if n >= 2:
                    round_u(0, n, True)
                if n:
                    gelu(0, n - 1)

            def step(I, r, more, first=False):
                m = BODY * I + r
                if more:
                    round_u(I + 1, r)
                act.wait_ge(v_in[r % RAW], 16 * (BODY // RAW * I + r // RAW + 1))
                if not (first and r < 2):
                    act.wait_ge(v_used, m - 1)
                nc.scalar.activation(v_hi[:, r % 2, :], v_raw[:, r % RAW, :], ACT.Copy).then_inc(v_hi_made, 1)
                act.wait_ge(w_made, m + 1)
                nc.scalar.activation(w_hi[:, r % 2, :], w_raw[:, r % 2, :], ACT.Copy).then_inc(w_hi_made, 1)
                if r == 0:
                    gelu(I, AHEAD - 1)
                elif more:
                    gelu(I + 1, r - 1)

            for r in range(BODY):
                step(0, r, True, True)
            gate_exps(NT - 1)
            with act.Fori(1, ITERS // 2) as I:
                for r in range(BODY):
                    step(I, r, True)
            act.wait_ge(dot_done, NSEL)
            nc.scalar.activation(act_w[:, :], act_w[:, :], ACT.Gelu).then_inc(gelu_done, 1)
            with act.Fori(ITERS // 2, ITERS - 1) as I:
                for r in range(BODY):
                    step(I, r, True)
            for r in range(BODY):
                step(ITERS - 1, r, False)

            for t in range(NT):
                act.wait_ge(x2_ready, t + 1)
                nc.scalar.activation(y[:, t, :], xs[:, t, :], ACT.Square, accum_out=x2_ss[:, t:t + 1]).then_inc(x2_squared, 1)
                act.wait_ge(x2_mean, t + 1)
                nc.scalar.activation(x2_rms[:, t:t + 1], x2_ss[:, t:t + 1], ACT.Sqrt).then_inc(x2_root, 1)

        @block.tensor
        def _(pe):
            def start(*name):
                b, n = place[name]
                if n > 1:
                    pe.wait_ge(read[b], n - 1)
                return bank[b]

            def done(ins, *name):
                ins.then_inc(full[place[name][0]], 1)

            def ada_row(g):
                pe.wait_ge(ada_summed, g + 1)
                b = start("ada", g)
                done(nc.tensor.matmul(b[:, :], ones, ada[:, g * HALF:(g + 1) * HALF], start=True, stop=True), "ada", g)

            def transposes(name, blocks):
                b = start(*name)
                for j, blk in enumerate(blocks):
                    ins = nc.tensor.transpose(b[:, j * P:(j + 1) * P], blk, ident[:, :])
                done(ins, *name)

            pe.wait_ge(made, 3)
            for g in range(4):
                ada_row(g)
            for t in range(NT):
                pe.wait_ge(h1_ready, t + 1)
                for s in range(2):
                    transposes(("h1T", t, s), [h1[:, t, (4 * s + j) * P:(4 * s + j + 1) * P] for j in range(4)])

            for g in ("zv", "v", "f", "zu"):
                if g == "f":
                    pe.wait_ge(fw_in, 16)
                    b = start("f")
                    for t in range(NT):
                        for k in range(KC):
                            ins = nc.tensor.matmul(b[:, t * HEADS:(t + 1) * HEADS], hT[:, k, t * P:(t + 1) * P],
                                                   f_w[:, k, :], start=(k == 0), stop=(k == KC - 1))
                    done(ins, "f")
                    continue
                w = wait_weights(pe, "w_in", g)
                for t in range(NT):
                    wait_read(pe, "h1T", t, 1)
                    wait_read(pe, "h1T", t, 0)
                    b = start(g, t)
                    for k in range(KC):
                        ins = nc.tensor.matmul(b[:, :], hT[:, k, t * P:(t + 1) * P], w[:, k, :],
                                               start=(k == 0), stop=(k == KC - 1))
                    done(ins, g, t)
            for g in ("q", "k"):
                w = wait_weights(pe, "w_in", g)
                for n in range(4):
                    b = start(g, n)
                    for k in range(KC):
                        ins = nc.tensor.matmul(b[:, :], w[:, k, n * P:(n + 1) * P], hT[:, k, :],
                                               start=(k == 0), stop=(k == KC - 1))
                    done(ins, g, n)
            for g in range(4, 12):
                ada_row(g)

            pe.wait_ge(f_done, 1)
            b = start("cum")
            for kt in range(NT):
                for st in range(kt + 1):
                    ins = nc.tensor.matmul(b[0:HEADS, kt * P:(kt + 1) * P], lsg[:, st * HEADS:(st + 1) * HEADS],
                                           tri if st == kt else ones, start=(st == 0), stop=(st == kt))
            done(ins, "cum")

            pe.wait_ge(sgw_masked, 1)
            pe.wait_ge(v_norm, 1)
            for n in range(4):
                b = start("sgu", n)
                for j in range(2):
                    h = 2 * n + j
                    ins = nc.tensor.matmul(b[:, j * 256:(j + 1) * 256].rearrange("p (t d) -> p t d", t=NT), sgw[:, h, :],
                                           y[:, :, HALF + h * DH:HALF + (h + 1) * DH], start=True, stop=True)
                done(ins, "sgu", n)

            def logits(n):
                qt, h = ATTN[n]
                keys = (qt + 1) * P
                b = start("S", n)
                nc.tensor.matmul(b[:, 0:keys], q_z[:, h, qt * P:(qt + 1) * P], kT[:, h // 2, 0:keys],
                                 start=True, stop=False)
                done(nc.tensor.matmul(b[:, 0:keys], ident[0:HEADS, h:h + 1].broadcast_to([HEADS, P]), ncum[:, 0:keys],
                                      start=False, stop=True), "S", n)

            def turn(n):
                qt, h = ATTN[n]
                wait_read(pe, "S", n)
                transposes(("PT", n), [p_exp[:, n % 2, kb * P:(kb + 1) * P] for kb in range(qt + 1)])

            def values(n):
                qt, h = ATTN[n]
                wait_read(pe, "PT", n)
                b = start("O", qt) if h == 0 else bank[place["O", qt][0]]
                for kb in range(qt + 1):
                    ins = nc.tensor.matmul(b[:, h * DH:(h + 1) * DH], p_T[:, n % 2, kb * P:(kb + 1) * P],
                                           v_tok[:, kb, h * DH:(h + 1) * DH], start=(kb == 0), stop=(kb == qt))
                if h == HEADS - 1:
                    done(ins, "O", qt)
                else:
                    ins.then_inc(pT_used, 1)

            wait_read(pe, "cum")
            wait_read(pe, "q", 3)
            wait_read(pe, "k", 3)
            wait_read(pe, "v", 3)
            for n in range(len(ATTN) + 2):
                if n < len(ATTN):
                    logits(n)
                if 1 <= n <= len(ATTN):
                    turn(n - 1)
                if n >= 2:
                    values(n - 2)

            for t in range(NT):
                pe.wait_ge(y_ready, t + 1)
                for s in range(2):
                    transposes(("yT", t, s), [y[:, t, (4 * s + j) * P:(4 * s + j + 1) * P] for j in range(4)])
            pe.wait_ge(w_out_gated, 2 * KC)
            for t in ORDER:
                wait_read(pe, "yT", t, 0)
                wait_read(pe, "yT", t, 1)
                for s in range(2):
                    w = weights[:, slot_of["w_out", s], :, :]
                    b = start("mix", t, s)
                    for k in range(KC):
                        ins = nc.tensor.matmul(b[:, :], yT[:, t, k, :], w[:, k, :], start=(k == 0), stop=(k == KC - 1))
                    done(ins, "mix", t, s)

            def turn_h2(t):
                pe.wait_ge(h2_ready, ORDER.index(t) + 1)
                for s in range(2):
                    transposes(("h2T", t, s), [y[:, t, (4 * s + j) * P:(4 * s + j + 1) * P] for j in range(4)])

            def query(n):
                t = ORDER[n]
                wait_read(pe, "h2T", t, 0)
                wait_read(pe, "h2T", t, 1)
                pe.wait_ge(keys_in, 16)
                for pair in QUERY_PAIRS:
                    for g in pair:
                        w = wait_weights(pe, "w_query", g)
                        b = start("qrow", n, g)
                        for k in range(KC):
                            ins = nc.tensor.matmul(b[:, :], h2T(t)[:, k, :], w[:, k, :], start=(k == 0), stop=(k == KC - 1))
                        done(ins, "qrow", n, g)
                    for g in pair:
                        wait_read(pe, "qrow", n, g)
                        transposes(("qT", n, g), [qrow(n)[:, (4 * g + j) * P:(4 * g + j + 1) * P] for j in range(4)])
                    for g in pair:
                        wait_read(pe, "qT", n, g)
                        b = start("score", n, g)
                        for j in range(4):
                            p = 4 * g + j
                            ins = nc.tensor.matmul(b[:, j * P:(j + 1) * P], qT(n)[:, p, :], keysT[:, p, :], start=True, stop=True)
                        done(ins, "score", n, g)

            def build(n):
                if n:
                    pe.wait_ge(build_read, n * BATCHES)
                pe.wait_ge(gates_ready, n + 1)
                transposes(("turn", n), [picks(n)[2], picks(n)[3], gate[:, :]])
                wait_read(pe, "turn", n)

                def batches(i, first):
                    for b in range(HOT):
                        m = n * BATCHES + HOT * i + b
                        pe.wait_ge(hot_gated, m + 1)
                        if not (first and b < 2):
                            pe.wait_ge(build_read, m - 1)
                        for q in range(BATCH):
                            ins = nc.tensor.matmul(bank[6 + b % 2][:, q * P:(q + 1) * P], hot_j[:, b, q, :], hot_i[:, b, q, :],
                                                   start=True, stop=True)
                        ins.then_inc(built, 1)

                if n == 0:
                    for s in range(2):
                        wait_read(pe, "h2T", ORDER[DENSE - 1], s)
                    batches(0, True)
                with pe.Fori(1 if n == 0 else 0, BATCHES // HOT) as i:
                    batches(i, False)

            turn_h2(ORDER[0])
            query(0)
            for t in ORDER[1:]:
                turn_h2(t)
            for n in range(DENSE):
                query(n + 1)
                build(n)

            def products(I, r, first=False):
                m = BODY * I + r
                pe.wait_ge(u_lo_made, m + 1)
                if not (first and r < 2):
                    pe.wait_ge(a_read, m - 1)
                a = bank[r % 2][:, 0:DTOK].rearrange("p (d t) -> p d t", d=DENSE)
                uh = u_hi[r % 2][:, :].rearrange("p (k e) -> p k e", k=KC)
                ul = u_lo[:, r % RAW, :].rearrange("p (k e) -> p k e", k=KC)
                for k in range(KC):
                    nc.tensor.matmul(a, uh[:, k, :], h2_hi[:, :, k, :], start=(k == 0), stop=False)
                    nc.tensor.matmul(a, uh[:, k, :], h2_lo[:, :, k, :], start=False, stop=False)
                    ins = nc.tensor.matmul(a, ul[:, k, :], h2_hi[:, :, k, :], start=False, stop=(k == KC - 1))
                ins.then_inc(a_full, 1)

            def outputs(I, r, begin, end):
                m = BODY * I + r
                pe.wait_ge(v_lo_made, m + 1)
                pe.wait_ge(w_lo_made, m + 1)
                for d in range(DENSE):
                    wh = w_hi[:, r % 2, d * P:(d + 1) * P]
                    wl = w_lo[:, r % 2, d * P:(d + 1) * P]
                    for s in range(2):
                        acc, cols = bank[2 + 2 * d + s][:, :], slice(s * HALF, (s + 1) * HALF)
                        nc.tensor.matmul(acc, wh, v_hi[:, r % 2, cols], start=begin, stop=False)
                        nc.tensor.matmul(acc, wh, v_lo[:, r % RAW, cols], start=False, stop=False)
                    for s in range(2):
                        acc, cols = bank[2 + 2 * d + s][:, :], slice(s * HALF, (s + 1) * HALF)
                        ins = nc.tensor.matmul(acc, wl, v_hi[:, r % 2, cols], start=False, stop=end)
                ins.then_inc(v_used, 1)

            pe.wait_ge(h2_lo_made, DENSE)
            for g in range(4):
                wait_read(pe, "score", NT - 1, g)
            for g in (2, 3):
                wait_read(pe, "qT", NT - 1, g)
            for n in range(AHEAD):
                products(0, n, True)
            pe.wait_ge(build_read, DENSE * BATCHES)
            for r in range(BODY):
                products(1, r)
                outputs(0, r, r == 0, False)
            with pe.Fori(1, ITERS - 1) as I:
                for r in range(BODY):
                    products(I + 1, r)
                    outputs(I, r, False, False)
            for r in range(BODY):
                outputs(ITERS - 1, r, False, r == BODY - 1)

        @block.vector
        def _(dve):
            links = [0]

            def link(ins):
                links[0] += 1
                ins.then_inc(v_chain, 1)
                dve.wait_ge(v_chain, links[0])

            tt, ts, stt = nc.vector.tensor_tensor, nc.vector.tensor_scalar, nc.vector.scalar_tensor_tensor

            dve.wait_ge(c_exped, 1)
            link(ts(c_exp, c_exp, 1.0, None, ALU.add))
            link(nc.vector.reciprocal(c_exp, c_exp))
            link(tt(c_act, c_col, c_exp, ALU.mult))

            def ada_sum(g):
                w = wait_weights(dve, "ada", g)
                acc = ada[:, g * HALF:(g + 1) * HALF]
                for k in range(KC):
                    ins = stt(out=acc, in0=w[:, k, :], scalar=c_act[:, k:k + 1], in1=acc, op0=ALU.mult, op1=ALU.add)
                    if k < KC - 1:
                        link(ins)
                ins.then_inc(ada_summed, 1)

            dve.wait_ge(b_ada_early, 16 * 4)
            for g in range(4):
                ada_sum(g)
            dve.wait_ge(x_squared, NT)
            ts(x_ss, x_ss, 1.0 / D, EPS, ALU.mult, ALU.add).then_inc(x_mean, 1)
            dve.wait_ge(x_root, 1)
            link(nc.vector.reciprocal(x_rms, x_rms))
            dve.wait_ge(made, 3)
            link(nc.vector.tensor_copy(iota16, iota_u))
            for g in range(4):
                wait_read(dve, "ada", g)
            dve.wait_ge(norm1_in, 16)
            stt(out=scale1, in0=scale1, scalar=1.0, in1=norm1_row, op0=ALU.add, op1=ALU.mult).then_inc(a1_done, 1)
            dve.wait_ge(a1_done, 1)
            for t in range(NT):
                link(stt(out=h1[:, t, :], in0=xs[:, t, :], scalar=x_rms[:, t:t + 1], in1=scale1, op0=ALU.mult, op1=ALU.mult))
                tt(h1[:, t, :], h1[:, t, :], shift1, ALU.add).then_inc(h1_ready, 1)
            for t in range(NT):
                b = wait_full(dve, "v", t)
                release(nc.vector.tensor_copy(v_tok[:, t, :], b[:, :]), "v", t)

            b = wait_full(dve, "f")
            dve.wait_ge(small_in, 48)
            ins = tt(logit.rearrange("p (t h) -> p t h", t=NT), b[:, 0:32].rearrange("p (t h) -> p t h", t=NT),
                     bf_row.unsqueeze(1).broadcast_to([P, NT, HEADS]), ALU.add)
            release(ins, "f")
            wait_read(dve, "f")
            stt(out=lsg_e, in0=logit, scalar=-1.0, in1=logit, op0=ALU.mult, op1=ALU.max).then_inc(f_abs, 1)
            dve.wait_ge(f_exp, 1)
            ts(lsg_e, lsg_e, 1.0, None, ALU.add).then_inc(f_plus, 1)
            dve.wait_ge(f_log, 1)
            stt(out=lsg, in0=logit, scalar=0.0, in1=lsg_e, op0=ALU.min, op1=ALU.subtract).then_inc(f_done, 1)

            zv = y[:, :, HALF:D].rearrange("p t (h d) -> p t h d", h=HEADS)

            def per_head(s):
                return s.rearrange("p (t h) -> p t h", t=NT)

            def over_head(s):
                return per_head(s).unsqueeze(3).broadcast_to([P, NT, HEADS, DH])

            wait_read(dve, "zv", NT - 1)
            link(nc.vector.tensor_reduce(per_head(v_mean), zv, AX_X, ALU.add))
            link(ts(v_mean, v_mean, -1.0 / DH, None, ALU.mult))
            for t in range(NT):
                ins = tt(zv[:, t], zv[:, t], per_head(v_mean)[:, t].unsqueeze(2).broadcast_to([P, HEADS, DH]), ALU.add)
            link(ins)
            sq = v_sq.rearrange("p (t d) -> p t d", t=2)
            for n in range(2):
                link(tt(sq, y[:, 2 * n:2 * n + 2, HALF:D], y[:, 2 * n:2 * n + 2, HALF:D], ALU.mult))
                link(nc.vector.tensor_reduce(v_var[:, 16 * n:16 * n + 16], v_sq.rearrange("p (g d) -> p g d", d=DH), AX_X, ALU.add))
            ts(v_var, v_var, 1.0 / DH, EPS, ALU.mult, ALU.add).then_inc(v_var_ready, 1)
            dve.wait_ge(b_ada_late, 16 * 8)
            for g in range(4, 7):
                ada_sum(g)
            for n in range(4):
                b = wait_full(dve, "k", n)
                release(nc.vector.tensor_copy(kT[:, n, :], b[:, :]), "k", n)
            dve.wait_ge(v_root, 1)
            link(nc.vector.reciprocal(v_var, v_var))
            for t in range(NT):
                ins = tt(zv[:, t], zv[:, t], per_head(v_var)[:, t].unsqueeze(2).broadcast_to([P, HEADS, DH]), ALU.mult)
            link(ins)
            dve.wait_ge(ln_in, 32)
            zvf = y[:, :, HALF:D]
            link(tt(zvf, zvf, ln_g.unsqueeze(1).broadcast_to([P, NT, HALF]), ALU.mult))
            tt(zvf, zvf, ln_b.unsqueeze(1).broadcast_to([P, NT, HALF]), ALU.add).then_inc(v_norm, 1)
            for g in range(7, 12):
                ada_sum(g)
            for g in range(8, 10):
                wait_read(dve, "ada", g)
            dve.wait_ge(norm2_in, 16)
            stt(out=scale2, in0=scale2, scalar=1.0, in1=norm2_row, op0=ALU.add, op1=ALU.mult).then_inc(a2_done, 1)

            wait_read(dve, "zu", NT - 1)
            for n in range(4):
                b = wait_full(dve, "sgu", n)
                for j in range(2):
                    h = 2 * n + j
                    zu = y[:, :, h * DH:(h + 1) * DH]
                    ins = stt(out=zu, in0=b[:, j * 256:(j + 1) * 256].rearrange("p (t d) -> p t d", t=NT),
                              scalar=sgb[:, h:h + 1], in1=zu, op0=ALU.add, op1=ALU.mult)
                release(ins, "sgu", n)

            def row_max(n):
                qt, h = ATTN[n]
                keys = (qt + 1) * P
                b = wait_full(dve, "S", n)
                own = b[:, qt * P:keys]
                link(tt(own, own, causal, ALU.add))
                nc.vector.tensor_reduce(nmax[:, n:n + 1], b[:, 0:keys], AX_X, ALU.max, negate=True).then_inc(neg_max, 1)

            def copy_turned(n):
                qt, h = ATTN[n]
                b = wait_full(dve, "PT", n)
                if n >= 2:
                    was_qt, was_h = ATTN[n - 2]
                    if was_h == HEADS - 1:
                        wait_full(dve, "O", was_qt)
                    else:
                        dve.wait_ge(pT_used, was_qt * (HEADS - 1) + was_h + 1)
                release(nc.vector.tensor_copy(p_T[:, n % 2, 0:(qt + 1) * P], b[:, 0:(qt + 1) * P]), "PT", n)

            def output(qt):
                b = wait_full(dve, "O", qt)
                rs = slice(qt * HEADS, (qt + 1) * HEADS)
                for n in (-2, -1):
                    wait_read(dve, "S", (qt + 1) * HEADS + n)
                link(nc.vector.reciprocal(o_scale[:, rs], rsum[:, rs]))
                release(tt(y[:, qt, HALF:D].rearrange("p (h d) -> p h d", h=HEADS),
                           b[:, :].rearrange("p (h d) -> p h d", h=HEADS),
                           o_scale[:, rs].unsqueeze(2).broadcast_to([P, HEADS, DH]), ALU.mult), "O", qt)

            dve.wait_ge(causal_made, 1)
            for n in range(len(ATTN) + 2):
                if n < len(ATTN):
                    row_max(n)
                if 1 <= n <= len(ATTN):
                    copy_turned(n - 1)
                if n >= 2 and ATTN[n - 2][1] == HEADS - 1:
                    output(ATTN[n - 2][0])

            def head_norm(t):
                dve.wait_ge(y_root, t + 1)
                link(nc.vector.reciprocal(y_rms[:, t], y_rms[:, t]))
                yh = y[:, t, :].rearrange("p (h d) -> p h d", d=DH)
                tt(yh, yh, y_rms[:, t].unsqueeze(2).broadcast_to([P, 2 * HEADS, DH]), ALU.mult).then_inc(y_ready, 1)

            def residual(t):
                for s in range(2):
                    b = wait_full(dve, "mix", t, s)
                    xh = xs[:, t, s * HALF:(s + 1) * HALF]
                    release(tt(xh, b[:, :], xh, ALU.add), "mix", t, s)

            def x1_stat(n):
                t = ORDER[n]
                dve.wait_ge(x1_squared, n + 1)
                ts(x1_ss[:, t:t + 1], x1_ss[:, t:t + 1], 1.0 / D, EPS, ALU.mult, ALU.add).then_inc(x1_mean, 1)

            def second_norm(n):
                t = ORDER[n]
                dve.wait_ge(x1_root, n + 1)
                link(nc.vector.reciprocal(x1_rms[:, t:t + 1], x1_rms[:, t:t + 1]))
                link(stt(out=y[:, t, :], in0=xs[:, t, :], scalar=x1_rms[:, t:t + 1], in1=scale2, op0=ALU.mult, op1=ALU.mult))
                tt(y[:, t, :], y[:, t, :], shift2, ALU.add).then_inc(h2_ready, 1)

            for t in range(NT):
                dve.wait_ge(y_squared, t + 1)
                link(nc.vector.tensor_reduce(y_var[:, t], squares[:, t, :].rearrange("p (h d) -> p h d", d=DH), AX_X, ALU.add))
                ts(y_var[:, t], y_var[:, t], 1.0 / DH, EPS, ALU.mult, ALU.add).then_inc(y_mean, 1)
            for t in range(NT):
                head_norm(t)
            for t in range(NT):
                for s in range(2):
                    b = wait_full(dve, "yT", t, s)
                    release(tt(yT[:, t, 4 * s:4 * s + 4, :], b[:, :].rearrange("p (k t) -> p k t", k=4),
                               out_g[:, 4 * s:4 * s + 4].unsqueeze(2).broadcast_to([P, 4, P]), ALU.mult), "yT", t, s)
            for n in range(NT + 2):
                if n < NT:
                    residual(ORDER[n])
                if 1 <= n <= NT:
                    x1_stat(n - 1)
                if n >= 2:
                    second_norm(n - 2)

            def top16(values_out, index_out, rows, groups):
                for g in range(groups):
                    ins = nc.vector.max(values_out[:, g, 0:8], rows[:, g, :])
                link(ins)
                for g in range(groups):
                    ins = nc.vector.max_index(index_out[:, g, 0:8], values_out[:, g, 0:8], rows[:, g, :])
                link(ins)
                yield
                for g in range(groups):
                    ins = nc.vector.match_replace(rows[:, g, :], values_out[:, g, 0:8], rows[:, g, :], TAKEN)
                link(ins)
                yield
                for g in range(groups):
                    ins = nc.vector.max(values_out[:, g, 8:16], rows[:, g, :])
                link(ins)
                for g in range(groups):
                    ins = nc.vector.max_index(index_out[:, g, 8:16], values_out[:, g, 8:16], rows[:, g, :])
                link(ins)

            def retrieve(n):
                cand = cand_of(n)
                pos_a, pos_b, sel_i, sel_j, pos_u = picks(n)
                for pair in QUERY_PAIRS:
                    for g in pair:
                        wait_read(dve, "score", n, g)
                    rows = slice(4 * pair[0], 4 * pair[-1] + 4)
                    yield from top16(top_v[:, rows], top_i[:, rows], scores(n)[:, rows], HP // 2)
                    yield
                halves_v = top_v.rearrange("p (h s) k -> p h s k", s=2)
                link(tt(cand.rearrange("p h (a b) -> p h a b", b=TOPK),
                        halves_v[:, :, 0, :].unsqueeze(3).broadcast_to([P, PH, TOPK, TOPK]),
                        halves_v[:, :, 1, :].unsqueeze(2).broadcast_to([P, PH, TOPK, TOPK]), ALU.add))
                yield from top16(best_v, best_p, cand, PH)
                yield
                if n:
                    wait_full(dve, "turn", n - 1)
                tt(gate[:, :].rearrange("p (h k) -> p h k", h=PH), best_v,
                   best_v[:, :, 0:1].broadcast_to([P, PH, TOPK]), ALU.subtract).then_inc(best_ready, 1)
                link(nc.vector.tensor_copy(top_f, top_i))
                flat_p = best_p.rearrange("p h k -> p (h k)")
                link(ts(pos_u.bitcast(U32), flat_p, 4, None, ALU.logical_shift_right))
                link(nc.vector.tensor_copy(pos_a, pos_u.bitcast(U32)))
                link(ts(pos_u.bitcast(U32), flat_p, 15, None, ALU.bitwise_and))
                link(nc.vector.tensor_copy(pos_b, pos_u.bitcast(U32)))

                def mark(c):
                    s, hh = PICKS[c]
                    tt(onehot(n, c), (pos_a, pos_b)[s][:, 64 * hh:64 * hh + 64].unsqueeze(2).broadcast_to([P, 64, TOPK]),
                       iota16.unsqueeze(1).broadcast_to([P, 64, TOPK]), ALU.is_equal).then_inc(picks_marked, 1)

                def sum_up(c):
                    s, hh = PICKS[c]
                    dve.wait_ge(picks_weighted, len(PICKS) * n + c + 1)
                    link(nc.vector.tensor_reduce((sel_i, sel_j)[s][:, 64 * hh:64 * hh + 64], onehot(n, c), AX_X, ALU.add))

                for c in range(3):
                    mark(c)
                sum_up(0)
                mark(3)
                yield
                for c in range(1, 4):
                    sum_up(c)
                if ORDER[n] == SPARSE:
                    stt(out=idx[:, 0, :], in0=sel_i, scalar=float(NKEYS), in1=sel_j, op0=ALU.mult, op1=ALU.add)\
                        .then_inc(topk_done, 1)

            def gates(n):
                dve.wait_ge(gate_exp, n + 1)
                gh = gate[:, :].rearrange("p (h k) -> p h k", h=PH)
                link(nc.vector.tensor_reduce(gate_sum, gh, AX_X, ALU.add))
                link(nc.vector.reciprocal(gate_sum, gate_sum))
                tt(gh, gh, gate_sum.unsqueeze(2).broadcast_to([P, PH, TOPK]), ALU.mult).then_inc(gates_ready, 1)

            def hot_rows(n, i, first):
                for b in range(HOT):
                    if not first:
                        dve.wait_ge(built, n * BATCHES + HOT * (i - 1) + b + 1)
                    for which, rows in ((1, hot_j), (0, hot_i)):
                        key = turned[:, n % 2, which, bass.ds((HOT * i + b) * BATCH, BATCH)]
                        ins = tt(rows[:, b], iota128.unsqueeze(1).broadcast_to([P, BATCH, P]),
                                 key.unsqueeze(2).broadcast_to([P, BATCH, P]), ALU.is_equal)
                    ins.then_inc(hot_made, 1)

            dve.wait_ge(h2_ready, NT)
            for n in range(DENSE):
                for _step in retrieve(n):
                    pass
                gates(n)
                wait_read(dve, "turn", n)
                if n == 0:
                    dve.wait_ge(iota_made, 2)
                    hot_rows(n, 0, True)
                with dve.Fori(1 if n == 0 else 0, BATCHES // HOT) as i:
                    hot_rows(n, i, False)

            wait_full(dve, "qrow", NT - 1, 0)
            for d in range(DENSE):
                dve.wait_ge(h2_hi_made, d + 1)
                tt(h2_lo[:, d], h2T(ORDER[d]), h2_hi[:, d].bitcast(F32), ALU.subtract).then_inc(h2_lo_made, 1)

            def rest_of_u(I, r):
                dve.wait_ge(u_hi_made, BODY * I + r + 1)
                tt(u_lo[:, r % RAW, :], u_raw[:, r % RAW, :], u_hi[r % 2][:, :].bitcast(F32), ALU.subtract).then_inc(u_lo_made, 1)

            steps = retrieve(NT - 1)
            for n in range(AHEAD):
                rest_of_u(0, n)
                next(steps, None)

            def sparse_rows(I, r, adding):
                for q in range(STEP_ROWS):
                    at = STEP_ROWS * r + q
                    per_body = STEP_ROWS * BODY
                    dve.wait_ge(gathered[at % ROWS], 16 * (per_body // ROWS * I + at // ROWS + 1))
                    gathered_row = ring(at % ROWS)
                    if not adding:
                        stt(out=gathered_row, in0=gathered_row, scalar=1.0, in1=y[:, SPARSE, :], op0=ALU.mult, op1=ALU.mult,
                            accum_out=act_w[:, bass.ds(per_body * I + at, 1)]).then_inc(dot_done, 1)
                        continue
                    n = per_body * (I - ITERS // 2) + at
                    dve.wait_ge(v_added, n + 1)
                    stt(out=y[:, SPARSE, :], in0=gathered_row, scalar=act_w[:, bass.ds(n, 1)], in1=y[:, SPARSE, :],
                        op0=ALU.mult, op1=ALU.add).then_inc(v_added, 1)

            def step(I, r, more, first, adding, rows=None):
                m = BODY * I + r
                if more:
                    rest_of_u(I + 1, r)
                dve.wait_ge(a_read, m + 1)
                if r % GLOAD == 0:
                    dve.wait_ge(g_in[r // GLOAD], 16 * (I + 1))
                if not (first and r < 2):
                    dve.wait_ge(v_used, m - 1)
                grouped = "p (g t) -> p g t"
                tt(w_raw[:, r % 2, :].rearrange(grouped, g=GROUPS), ahead[:, r, :].rearrange(grouped, g=GROUPS),
                   g_block[:, r // GLOAD, :, r % GLOAD, :], ALU.mult).then_inc(w_made, 1)
                dve.wait_ge(v_hi_made, m + 1)
                tt(v_lo[:, r % RAW, :], v_raw[:, r % RAW, :], v_hi[:, r % 2, :].bitcast(F32), ALU.subtract).then_inc(v_lo_made, 1)
                dve.wait_ge(w_hi_made, m + 1)
                tt(w_lo[:, r % 2, :], w_raw[:, r % 2, :], w_hi[:, r % 2, :].bitcast(F32), ALU.subtract).then_inc(w_lo_made, 1)
                for at in [r] if rows is None else rows:
                    sparse_rows(I, at, adding)

            for r in range(BODY // 2):
                step(0, r, True, True, False, rows=[])
                next(steps, None)
            for _step in steps:
                pass
            for r in range(BODY // 2, BODY):
                step(0, r, True, True, False, rows=[2 * r - BODY, 2 * r - BODY + 1])
            gates(NT - 1)
            with dve.Fori(1, ITERS // 2) as I:
                for r in range(BODY):
                    step(I, r, True, False, False)
            dve.wait_ge(gelu_done, 1)
            tt(act_w[:, :], act_w[:, :], gate[:, :], ALU.mult).then_inc(w_ready, 1)
            dve.wait_ge(dot_done, NSEL)
            dve.wait_ge(w_ready, 1)
            nc.vector.memset(y[:, SPARSE, :], 0.0).then_inc(v_added, 1)
            with dve.Fori(ITERS // 2, ITERS - 1) as I:
                for r in range(BODY):
                    step(I, r, True, False, True)
            for r in range(BODY):
                step(ITERS - 1, r, False, False, True)

            def finish(t):
                dve.wait_ge(x2_squared, t + 1)
                ts(x2_ss[:, t:t + 1], x2_ss[:, t:t + 1], 1.0 / D, EPS, ALU.mult, ALU.add).then_inc(x2_mean, 1)
                dve.wait_ge(x2_root, t + 1)
                link(nc.vector.reciprocal(x2_rms[:, t:t + 1], x2_rms[:, t:t + 1]))
                stt(out=xs[:, t, :], in0=xs[:, t, :], scalar=x2_rms[:, t:t + 1], in1=final_row[:, :], op0=ALU.mult, op1=ALU.mult)\
                    .then_inc(out_ready, 1)

            dve.wait_ge(final_in, 16)
            dve.wait_ge(v_added, NSEL + 1)
            for t in range(NT):
                if t == SPARSE:
                    link(tt(y[:, t, :], y[:, t, :], gate2, ALU.mult))
                else:
                    dve.wait_ge(v_used, NKEYS)
                    for s in range(2):
                        cols = slice(s * HALF, (s + 1) * HALF)
                        ins = tt(y[:, t, cols], bank[2 + 2 * ORDER.index(t) + s][:, :], gate2[:, cols], ALU.mult)
                    link(ins)
                tt(xs[:, t, :], xs[:, t, :], y[:, t, :], ALU.add).then_inc(x2_ready, 1)
                if t:
                    finish(t - 1)
            finish(NT - 1)


def kernel(x, c, w_ada, b_ada, norm1_g, w_in, b_f, sg_ln_g, sg_ln_b, sg_w, sg_b, out_g_sg, out_g_fox,
           w_out, norm2_g, w_query, sub_keys, expert_u, expert_v, final_g):
    import concourse.bacc as bacc
    import numpy as np
    from concourse.bass_utils import run_bass_kernel_spmd

    laid_out = {
        "x": x[0], "cT": np.transpose(c.reshape(KC, P)), "w_ada": w_ada[0], "b_ada": b_ada[0], "norm1_g": norm1_g[0], "w_in": w_in[0],
        "b_f": b_f[0], "sg_ln_g": sg_ln_g[0], "sg_ln_b": sg_ln_b[0],
        "sg_wT": np.transpose(sg_w[0], (2, 0, 1)),
        "sg_bT": np.transpose(sg_b[0]),
        "out_gT": np.transpose(np.concatenate([out_g_sg[0], out_g_fox[0]]).reshape(KC, P)), "w_out": w_out[0], "norm2_g": norm2_g[0],
        "w_query": w_query[0],
        "sub_keysT": np.transpose(sub_keys[0].reshape(HP, NKEYS, P), (2, 0, 1)),
        "uT": np.transpose(expert_u[0].reshape(NKEYS, NKEYS, KC, P), (0, 3, 2, 1)).reshape(NKEYS, P, D),
        "expert_u": expert_u[0], "expert_v": expert_v[0], "final_g": final_g,
    }
    nc = bacc.Bacc("TRN2", target_bir_lowering=False, num_devices=1)
    arrays, args = {}, []
    for name, a in laid_out.items():
        a = np.ascontiguousarray(a)
        arrays[f"in_{name}"] = a
        args.append(nc.dram_tensor(f"in_{name}", a.shape, mybir.dt.from_np(a.dtype), kind="ExternalInput").ap())
    args.append(nc.dram_tensor("out", (SEQ, D), F32, kind="ExternalOutput").ap())
    program(nc, *args)
    result = run_bass_kernel_spmd(nc, [arrays], core_ids=[0])
    return result.results[0]["out"].reshape(1, SEQ, D)
```
